# Optimizing a Trainium2 kernel written in Bass

```python
import math
import jax, jax.numpy as jnp
from jax import lax
import numpy as np

D_MODEL = 1024
BATCH = 1
SEQ = 256
DEPTH = 1

CONV_CH = 512
CONV_WIDTH = 31
N_HEADS = 8
HEAD_DIM = 64
ATTN_W = N_HEADS * HEAD_DIM
MOBA_BLOCK = 256
MOBA_TOPK = 3
Q_CHUNK = 128
N_EXPERTS = 32
TOP_K = 4
D_FF = D_MODEL
SWIGLU_LIMIT = 7.0
SWIGLU_ALPHA = 1.702
MOE_ROWS = 256
N_IN = 2 * CONV_CH + 3 * ATTN_W + 2 * D_MODEL
EPS = 1e-6

kernel_name = "hybrid_conformer_moba_moe_block"

def rms_norm(x, g):
    xf = x.astype(jnp.float32)
    y = xf * lax.rsqrt(jnp.mean(xf * xf, axis=-1, keepdims=True) + EPS)
    return (y * g.astype(jnp.float32)).astype(x.dtype)

def layer_norm(x, g, b):
    xf = x.astype(jnp.float32)
    mu = jnp.mean(xf, axis=-1, keepdims=True)
    var = jnp.mean(jnp.square(xf - mu), axis=-1, keepdims=True)
    y = (xf - mu) * lax.rsqrt(var + EPS)
    return (y * g.astype(jnp.float32) + b.astype(jnp.float32)).astype(x.dtype)

def alibi_slopes():
    return 2.0 ** (-8.0 * jnp.arange(1, N_HEADS + 1, dtype=jnp.float32) / N_HEADS)

def conformer_conv(u, dw, dw_b, ln_g, ln_b, w_o):
    a, g = jnp.split(u, 2, axis=-1)
    h = a * jax.nn.sigmoid(g)
    h = lax.conv_general_dilated(
        h, dw[:, None, :].astype(h.dtype), window_strides=(1,),
        padding=[(CONV_WIDTH - 1, 0)],
        dimension_numbers=("NWC", "WIO", "NWC"),
        feature_group_count=CONV_CH) + dw_b
    h = jax.nn.silu(layer_norm(h, ln_g, ln_b))
    return h @ w_o

def moba_attention(q, k, v, q_g, k_g):
    B, S = q.shape[0], q.shape[1]
    q = rms_norm(q, q_g).transpose(0, 2, 1, 3)
    k = rms_norm(k, k_g).transpose(0, 2, 1, 3)
    v = v.transpose(0, 2, 1, 3)
    nb = -(-S // MOBA_BLOCK)
    pad = nb * MOBA_BLOCK - S
    k = jnp.pad(k, ((0, 0), (0, 0), (0, pad), (0, 0)))
    v = jnp.pad(v, ((0, 0), (0, 0), (0, pad), (0, 0)))
    kb = k.reshape(B, N_HEADS, nb, MOBA_BLOCK, HEAD_DIM)
    vb = v.reshape(B, N_HEADS, nb, MOBA_BLOCK, HEAD_DIM)
    kmean = jnp.mean(kb, axis=3)
    topk = min(MOBA_TOPK, nb)
    slopes = alibi_slopes()
    scale = HEAD_DIM ** -0.5
    bi = jnp.arange(B)[:, None, None, None]
    hi = jnp.arange(N_HEADS)[None, :, None, None]
    blk_ids = jnp.arange(nb)
    kpos = jnp.arange(MOBA_BLOCK)

    def chunk(c):
        t0 = c * Q_CHUNK
        qc = lax.dynamic_slice_in_dim(q, t0, Q_CHUNK, axis=2)
        t = t0 + jnp.arange(Q_CHUNK)
        own = t0 // MOBA_BLOCK
        gate = jnp.einsum("bhqd,bhnd->bhqn", qc, kmean).astype(jnp.float32)
        gate = jnp.where(blk_ids < own, gate, -jnp.inf)
        _, sel = lax.top_k(gate, topk)
        sel_ok = sel < own
        ks = kb[bi, hi, sel]
        vs = vb[bi, hi, sel]
        s_past = jnp.einsum("bhqd,bhqrkd->bhqrk", qc, ks).astype(jnp.float32) * scale
        dist_past = (t[None, None, :, None, None] - (sel[..., None] * MOBA_BLOCK + kpos)).astype(jnp.float32)
        s_past = s_past - slopes[None, :, None, None, None] * dist_past
        s_past = jnp.where(sel_ok[..., None], s_past, -jnp.inf)
        ko = lax.dynamic_index_in_dim(kb, own, axis=2, keepdims=False)
        vo = lax.dynamic_index_in_dim(vb, own, axis=2, keepdims=False)
        s_own = jnp.einsum("bhqd,bhkd->bhqk", qc, ko).astype(jnp.float32) * scale
        dist_own = t[:, None] - (own * MOBA_BLOCK + kpos)[None, :]
        s_own = jnp.where(dist_own[None, None] >= 0,
                          s_own - slopes[None, :, None, None] * dist_own.astype(jnp.float32)[None, None],
                          -jnp.inf)
        s = jnp.concatenate([s_past.reshape(B, N_HEADS, Q_CHUNK, topk * MOBA_BLOCK), s_own], axis=-1)
        p = jax.nn.softmax(s, axis=-1).astype(v.dtype)
        p_past = p[..., :topk * MOBA_BLOCK].reshape(B, N_HEADS, Q_CHUNK, topk, MOBA_BLOCK)
        p_own = p[..., topk * MOBA_BLOCK:]
        return (jnp.einsum("bhqrk,bhqrkd->bhqd", p_past, vs)
                + jnp.einsum("bhqk,bhkd->bhqd", p_own, vo))

    out = lax.map(chunk, jnp.arange(S // Q_CHUNK))
    return out.transpose(1, 0, 3, 2, 4).reshape(B, S, ATTN_W)

def moe_ffn(xf, w_router, b_router, w_ug, b_ug, w_down, b_down):
    T = xf.shape[0]
    logits = (xf @ w_router + b_router).astype(jnp.float32)
    top_v, top_i = lax.top_k(logits, TOP_K)
    gates = jax.nn.softmax(top_v, axis=-1)
    n_assign = T * TOP_K
    flat_e = top_i.reshape(-1)
    flat_t = jnp.arange(n_assign, dtype=jnp.int32) // TOP_K
    flat_g = gates.reshape(-1)
    order = jnp.argsort(flat_e)
    se = flat_e[order]
    counts = jnp.bincount(flat_e, length=N_EXPERTS)
    starts = jnp.cumsum(counts) - counts
    padded = (counts + MOE_ROWS - 1) // MOE_ROWS * MOE_ROWS
    pad_end = jnp.cumsum(padded)
    pad_start = pad_end - padded
    dest = pad_start[se] + jnp.arange(n_assign) - starts[se]
    n_blocks = -(-n_assign // MOE_ROWS) + N_EXPERTS
    n_rows = n_blocks * MOE_ROWS
    row_tok = jnp.zeros((n_rows,), jnp.int32).at[dest].set(flat_t[order])
    row_gate = jnp.zeros((n_rows,), jnp.float32).at[dest].set(flat_g[order])
    blk_e = jnp.minimum(jnp.searchsorted(pad_end, jnp.arange(n_blocks) * MOE_ROWS, side="right"),
                        N_EXPERTS - 1)

    def run(args):
        tok, g, e = args
        h = xf[tok] @ w_ug[e] + b_ug[e]
        a = jnp.minimum(h[:, :D_FF], SWIGLU_LIMIT)
        lin = jnp.clip(h[:, D_FF:], -SWIGLU_LIMIT, SWIGLU_LIMIT)
        act = a * jax.nn.sigmoid(SWIGLU_ALPHA * a) * (lin + 1.0)
        y = act @ w_down[e] + b_down[e]
        return y * g[:, None].astype(y.dtype)

    ys = lax.map(run, (row_tok.reshape(n_blocks, MOE_ROWS),
                       row_gate.reshape(n_blocks, MOE_ROWS), blk_e))
    return jnp.zeros_like(xf).at[row_tok].add(ys.reshape(n_rows, -1))

def setup_inputs(seed: int = 0) -> dict:
    key = jax.random.key(seed)
    ks = jax.random.split(key, 20)
    L, D, C, A, E, F = DEPTH, D_MODEL, CONV_CH, ATTN_W, N_EXPERTS, D_FF
    n = jax.random.normal
    f32 = jnp.float32
    return {
        "x": n(ks[0], (BATCH, SEQ, D), f32),
        "norm1_g": 1.0 + 0.01 * n(ks[1], (L, D), f32),
        "w_in": n(ks[2], (L, D, N_IN), f32) * D ** -0.5,
        "b_gates": 0.01 * n(ks[3], (L, 2 * D), f32),
        "conv_dw": n(ks[4], (L, CONV_WIDTH, C), f32) * CONV_WIDTH ** -0.5,
        "conv_dw_b": 0.01 * n(ks[5], (L, C), f32),
        "conv_ln_g": 1.0 + 0.01 * n(ks[6], (L, C), f32),
        "conv_ln_b": 0.01 * n(ks[7], (L, C), f32),
        "w_conv_out": n(ks[8], (L, C, D), f32) * C ** -0.5,
        "q_norm_g": 1.0 + 0.01 * n(ks[9], (L, HEAD_DIM), f32),
        "k_norm_g": 1.0 + 0.01 * n(ks[10], (L, HEAD_DIM), f32),
        "w_attn_out": n(ks[11], (L, A, D), f32) * A ** -0.5,
        "w_out": n(ks[12], (L, D, D), f32) * D ** -0.5,
        "norm2_g": 1.0 + 0.01 * n(ks[13], (L, D), f32),
        "w_router": n(ks[14], (L, D, E), f32) * D ** -0.5,
        "b_router": 0.01 * n(ks[15], (L, E), f32),
        "w_up_gate": n(ks[16], (L, E, D, 2 * F), f32) * D ** -0.5,
        "b_up_gate": 0.01 * n(ks[17], (L, E, 2 * F), f32),
        "w_down": n(ks[18], (L, E, F, D), f32) * F ** -0.5,
        "b_down": 0.01 * n(ks[19], (L, E, D), f32),
    }

def reference(x, norm1_g, w_in, b_gates, conv_dw, conv_dw_b, conv_ln_g, conv_ln_b, w_conv_out,
              q_norm_g, k_norm_g, w_attn_out, w_out, norm2_g, w_router, b_router,
              w_up_gate, b_up_gate, w_down, b_down):
    B, S, D = x.shape
    h = x
    c1 = 2 * CONV_CH
    c2 = c1 + ATTN_W
    c3 = c2 + ATTN_W
    c4 = c3 + ATTN_W
    for l in range(DEPTH):
        u = rms_norm(h, norm1_g[l])
        proj = u @ w_in[l]
        y_conv = conformer_conv(proj[..., :c1], conv_dw[l], conv_dw_b[l],
                                conv_ln_g[l], conv_ln_b[l], w_conv_out[l])
        q = proj[..., c1:c2].reshape(B, S, N_HEADS, HEAD_DIM)
        k = proj[..., c2:c3].reshape(B, S, N_HEADS, HEAD_DIM)
        v = proj[..., c3:c4].reshape(B, S, N_HEADS, HEAD_DIM)
        y_attn = moba_attention(q, k, v, q_norm_g[l], k_norm_g[l]) @ w_attn_out[l]
        g = jax.nn.sigmoid(proj[..., c4:] + b_gates[l])
        mixed = g[..., :D] * y_conv + g[..., D:] * y_attn
        h = h + mixed @ w_out[l]
        u2 = rms_norm(h, norm2_g[l]).reshape(B * S, D)
        h = h + moe_ffn(u2, w_router[l], b_router[l], w_up_gate[l], b_up_gate[l],
                        w_down[l], b_down[l]).reshape(B, S, D)
    return h


_drawn_inputs = setup_inputs


def setup_inputs(seed=0):
    import zlib

    import numpy as np

    out = dict(_drawn_inputs(seed))
    spreads = {}
    factors = {'norm1_g': 2.987,
     'b_gates': 8.0,
     'conv_dw_b': 8.72,
     'conv_ln_g': 68.217,
     'conv_ln_b': 76.35,
     'q_norm_g': 22.674,
     'k_norm_g': 8.0,
     'b_router': 10.332,
     'b_up_gate': 25.768,
     'b_down': 95.153,
     'norm2_g': 12.052}
    for name, (base, spread) in spreads.items():
        noise = np.random.default_rng([zlib.crc32(name.encode()), seed]).standard_normal(out[name].shape)
        drawn = base * np.exp(spread * noise) if base else spread * noise
        out[name] = __import__('jax').numpy.asarray(drawn.astype(out[name].dtype))
    for name, factor in factors.items():
        out[name] = (out[name] * factor).astype(out[name].dtype)
    return out
```

```python
import concourse.bass as bass
from concourse import mybir
from contextlib import ExitStack

F32 = mybir.dt.float32
I32 = mybir.dt.int32
U32 = mybir.dt.uint32
ALU = mybir.AluOpType
ACT = mybir.ActivationFunctionType
AX = mybir.AxisListType

P = 128
T = 256
MT = T // P
D = 1024
KD = D // P
CC = 512
KC = CC // P
TAPS = 31
HEADS = 8
HD = 64
E = 32
TOPK = 4
FF = 1024
LIMIT = 7.0
ALPHA = 1.702
EPS = 1e-6
SLOTS = 64
MAX_TILES = T // SLOTS
GROUPS = 9
FAR = 1e30


def hybrid_block(nc, x, norm1_g, w_in, b_gates, conv_dw, conv_dw_b, conv_ln_g, conv_ln_b, w_conv_out,
                 q_norm_g, k_norm_g, w_attn_out, w_out, norm2_g, w_router, b_router,
                 w_up_gate, b_up_gate, w_down, b_down, out):
    ctx = ExitStack()
    with ctx:
        def sb(name, shape, dt=F32):
            return ctx.enter_context(nc.sbuf_tensor(name, shape, dt))

        def sem(name):
            return ctx.enter_context(nc.semaphore(name))

        UP_EVEN = sb("up_even", [P, KD * 2 * FF])
        UP_ODD = sb("up_odd", [P, KD * 2 * FF])
        DOWN = sb("down", [P, KD * D])
        up = [r[:, :].rearrange("p (k n) -> p k n", k=KD) for r in (UP_EVEN, UP_ODD)]
        down = DOWN[:, :].rearrange("p (k n) -> p k n", k=KD)
        REG_H = sb("reg_h", [P, 2048])
        REG_U = sb("reg_u", [P, 2048])
        REG_E = sb("reg_e", [P, 4096])
        REG_R = sb("reg_r", [P, 1152])

        slots = [REG_E[:, :], DOWN[:, 0:4096], DOWN[:, 4096:8192]]

        def tmp(at, n, **kw):
            v = UP_ODD[:, at:at + n]
            return v.rearrange("p (a b) -> p a b", **kw) if kw else v

        gates = tmp(0, 4096, a=16)
        xn = tmp(0, 2048, a=MT)
        junk = tmp(2048, 1024)
        aT = tmp(4096, 1024, a=KC)
        aoT = tmp(4096, 1024, a=KC)
        hp = tmp(5120, KC * (T + TAPS - 1), a=KC)
        cv = tmp(6272, 1024, a=KC)
        xc = tmp(7296, 1024, a=KC)
        sq = tmp(8320, 1024, a=KC)
        qn = tmp(9344, 1024, a=MT)
        kn = tmp(10368, 1024, a=MT)
        vv = tmp(11392, 1024, a=MT)
        qT = tmp(12416, 1024, a=KC)
        kT = tmp(13440, 1024, a=KC)
        dist = tmp(14464, 384)
        pT = [tmp(14848 + 384 * i, 384, a=3) for i in range(2)]
        rstd_c = tmp(15616, 256)
        std_c = tmp(15872, 256)
        prod = sq[:, 0:2, :]

        hx = REG_H[:, :].rearrange("p (m d) -> p m d", m=MT)
        uT = REG_U[:, :].rearrange("p (k t) -> p k t", k=KD)
        mixT = uT
        u2T = uT
        u2 = REG_E[:, 0:2048].rearrange("p (m d) -> p m d", m=MT)
        bup = REG_E[0:E, 2048:4096]
        rows = REG_R[0:46, 512:640]
        dwr = REG_R[0:TAPS, 0:512]
        sc = [REG_R[:, 384 * i:384 * i + 384] for i in range(2)]
        junk2 = REG_R[:, 0:512]
        eq = REG_R[:, 896:1024].rearrange("p (j e) -> p j e", j=TOPK)
        cumf = REG_R[0:1, 1024:1024 + 2 * (E + 1)]

        ACT_A, ACT_B, ACT_C, YS = [REG_H[:, 512 * i:512 * i + 512] for i in range(4)]
        gT = REG_H[0:E, 512:768]
        actT = REG_U[:, 0:512].rearrange("p (i s) -> p i s", i=4)
        XT = REG_R[:, 0:512].rearrange("p (k s) -> p k s", k=KD)
        hot = REG_R[:, 512:640].rearrange("p (m s) -> p m s", m=MT)
        hotg = REG_R[:, 640:896].rearrange("p (m s) -> p m s", m=MT)
        hotT = REG_R[:, 896:1152].rearrange("p (m t) -> p m t", m=MT)
        outs = UP_EVEN[:, 0:2048].rearrange("p (m d) -> p m d", m=MT)

        bdown = sb("bdown", [E, D])
        wr = sb("wr", [P, KD, E])
        ident = sb("ident", [P, P])
        tri = sb("tri", [P, P])
        ones = sb("ones", [P, P])
        iota = sb("iota", [P, T])
        par = sb("par", [P, 46])
        dwT = sb("dwT", [P, KC, TAPS])
        epst = sb("epst", [P, 1])
        st = sb("st", [P, 24])
        ssqk = sb("ssqk", [P, 2 * MT * HEADS])
        rqk = sb("rqk", [P, 2 * MT * HEADS])
        mx = sb("mx", [P, 2, 2])
        nmx = sb("nmx", [P, 2, 2])
        sm = sb("sm", [P, 2, 2])
        rsm = sb("rsm", [P, 2, 2])
        brt = sb("brt", [P, E])
        lg = sb("lg", [P, MT, E])
        top = sb("top", [P, MT, 8])
        topi = sb("topi", [P, MT, 8], U32)
        topf = sb("topf", [P, MT, 8])
        gt4 = sb("gt4", [P, MT, TOPK])
        gate = sb("gate", [P, MT, E])
        msk = sb("msk", [P, MT, E])
        pos = sb("pos", [P, MT, E])
        cnt = sb("cnt", [1, 3, E])
        cum = sb("cum", [1, 2 * (E + 1)], I32)
        sel = sb("sel", [E, SLOTS])

        g1c, g2c = par[:, 0:8], par[:, 8:16]
        bgc, dwb, lng, lnb = par[:, 16:32], par[:, 32:36], par[:, 36:40], par[:, 40:44]
        qg, kg = par[:, 44:45], par[:, 45:46]

        bank = [ctx.enter_context(nc.psum_tensor(f"bank{i}", [P, 512], F32)) for i in range(8)]
        HG, HL, GA, YB = bank[0:4]
        S_BANKS, T_BANK, O_BANK = bank[4:6], bank[6], bank[7]
        acc = bank[4:8]

        x_in, par_in, small_in, bup_in, out_sem = [sem(n) for n in ("x_in", "par_in", "small_in", "bup_in", "out_sem")]
        slot_in = [sem(f"slot_in{i}") for i in range(3)]
        w_used = sem("w_used")
        up_in = [[sem(f"up_in{a}_{c}") for c in range(KD)] for a in range(2)]
        down_in = [sem(f"down_in{c}") for c in range(4)]
        bank_full = [sem(f"bank_full{i}") for i in range(4)]
        bank_free = [sem(f"bank_free{i}") for i in range(4)]
        pool_const, pool_qk, pool_p = sem("pool_const"), sem("pool_qk"), sem("pool_p")
        act_step, dve_step, pool_step = sem("act_step"), sem("dve_step"), sem("pool_step")
        xn_ready, uT_ready = sem("xn_ready"), sem("uT_ready")
        qkT_full, qkT_ready = sem("qkT_full"), sem("qkT_ready")
        ssx, qk_std, rqk_ready = sem("ssx"), sem("qk_std"), sem("rqk_ready")
        a_ready, sg_ready, q_copied, v_copied = [sem(n) for n in ("a_ready", "sg_ready", "q_copied", "v_copied")]
        s_full, s_read, t_full, t_read, o_full, o_read = [sem(n) for n in ("s_full", "s_read", "t_full", "t_read", "o_full", "o_read")]
        nmx_ready, exp_done, rsm_ready, pv_done = [sem(n) for n in ("nmx_ready", "exp_done", "rsm_ready", "pv_done")]
        cv_done, xc_ready, sqr_ready, std_ready, z_ready, sig_ready, cT_ready = [
            sem(n) for n in ("cv_done", "xc_ready", "sqr_ready", "std_ready", "z_ready", "sig_ready", "cT_ready")]
        gates_pre, gates_ready, mix_ready = [sem(n) for n in ("gates_pre", "gates_ready", "mix_ready")]
        ss2, std2, u2_ready, u2T_ready, v0_ready, expg, tab_ready, gTf, gT_ready, cum_ready = [
            sem(n) for n in ("ss2", "std2", "u2_ready", "u2T_ready", "v0_ready", "expg", "tab_ready", "gTf", "gT_ready", "cum_ready")]
        seeded = sem("seeded")
        hot_ready, gathered, xt_ready, hotT_full, scattered, hotT_ready = [
            sem(n) for n in ("hot_ready", "gathered", "xt_ready", "hotT_full", "scattered", "hotT_ready")]
        up_done, down_done, h_free, clip_ready, sigm_ready, act_ready, actT_full, actT_ready, y_ready, moe_step = [
            sem(n) for n in ("up_done", "down_done", "h_free", "clip_ready", "sigm_ready", "act_ready", "actT_full",
                             "actT_ready", "y_ready", "moe_step")]
        out_left, out_right = sem("out_left"), sem("out_right")

        block = ctx.enter_context(nc.Block())

        win = w_in.rearrange("(k p) n -> p k n", p=P)
        stream = [(win[:, :, 512 * i:512 * i + 512], slots[i % 3].rearrange("p (k n) -> p k n", k=KD))
                  for i in range(GROUPS)]
        ATT_W, CONV_W, OUT_W = GROUPS, GROUPS + 1, GROUPS + 2
        stream.append((w_attn_out.rearrange("(k p) n -> p k n", p=P),
                       slots[ATT_W % 3].rearrange("p (k n) -> p k n", k=KC)))
        stream.append((w_conv_out.rearrange("(k p) n -> p k n", p=P),
                       slots[CONV_W % 3].rearrange("p (k n) -> p k n", k=KC)))
        wout = w_out.rearrange("(k p) n -> p k n", p=P)
        for half in range(2):
            stream.append((wout[:, :, 512 * half:512 * half + 512],
                           slots[(OUT_W + half) % 3].rearrange("p (k n) -> p k n", k=KD)))

        U_PAR = 0
        U_XT = 1
        U_G = U_XT + 4
        U_MEAN = U_G + 2 * GROUPS
        U_ATT = U_MEAN + 1
        U_VAR = U_ATT + 4
        U_CONV = U_VAR + 1
        U_OUT = U_CONV + 4
        U_U2T = U_OUT + 4
        U_LOG = U_U2T + 4
        U_TAB = U_LOG + 1
        U_GT = U_TAB + 1
        USES = U_GT + 1

        LAST_USE = [U_G + 2 * i + 1 for i in range(GROUPS)] + [U_ATT + 3, U_CONV + 3, U_OUT + 1, U_OUT + 3]

        def full(eng, u):
            eng.wait_ge(bank_full[u % 4], u // 4 + 1)

        def freed(eng, u):
            eng.wait_ge(bank_free[u % 4], u // 4 + 1)

        def used(eng, i):
            full(eng, LAST_USE[i])

        @block.sync
        def _(sp):
            sp.dma_start(hx, x.rearrange("(m p) d -> p m d", p=P)).then_inc(x_in, 16)

            def load_up(par_, c, e):
                sp.dma_start(up[par_][:, c, :], w_up_gate[e, c * P:(c + 1) * P, :]).then_inc(up_in[par_][c], 16)

            def load_down(c, e):
                sp.dma_start(down[:, 2 * c:2 * c + 2, :],
                             w_down[e, 2 * c * P:(2 * c + 2) * P, :].rearrange("(r p) n -> p r n", p=P)
                             ).then_inc(down_in[c], 16)

            for i, (src, dst) in enumerate(stream):
                if i >= 3:
                    used(sp, i - 3)
                sp.dma_start(dst, src).then_inc(slot_in[i % 3], 16)
                if 3 <= i < 3 + KD:
                    load_up(0, i - 3, 0)
            sp.wait_ge(mix_ready, 4)
            for c in range(KD):
                load_up(1, c, 1)
            used(sp, CONV_W)
            load_down(0, 0)
            load_down(1, 0)
            used(sp, OUT_W)
            load_down(2, 0)
            load_down(3, 0)
            used(sp, OUT_W + 1)
            sp.dma_start(bup, b_up_gate).then_inc(bup_in, 16)
            sp.wait_ge(cum_ready, 1)
            with sp.Fori(1, E // 2) as pair:
                for a in range(2):
                    e = sp.snap(2 * pair + a)
                    last2 = sp.value_load(cum[0:1, bass.ds(e + (E - 1), 1)], min_val=0, max_val=63)
                    last1 = sp.value_load(cum[0:1, bass.ds(e + E, 1)], min_val=0, max_val=63)
                    for c in range(KD):
                        sp.wait_ge(up_done, last2 * KD + (c + 1))
                        sp.dma_start(up[a][:, c, :],
                                     w_up_gate[bass.ds(e, 1), c * P:(c + 1) * P, :].rearrange("e p n -> p (e n)")
                                     ).then_inc(up_in[a][c], 16)
                    for c in range(4):
                        sp.wait_ge(down_done, last2 * 4 + (c + 1))
                        sp.dma_start(down[:, 2 * c:2 * c + 2, :],
                                     w_down[bass.ds(e - 1, 1), 2 * c * P:(2 * c + 2) * P, :].rearrange(
                                         "e (r p) n -> p (e r) n", p=P)).then_inc(down_in[c], 16)
            tail = sp.value_load(cum[0:1, 2 * E - 1:2 * E], min_val=0, max_val=63)
            for c in range(4):
                sp.wait_ge(down_done, tail * 4 + (c + 1))
                load_down(c, E - 1)
            for m in range(MT):
                sp.wait_ge(out_left, m + 1)
                sp.wait_ge(out_right, m + 1)
                sp.dma_start(out[m * P:(m + 1) * P, :], outs[:, m, :]).then_inc(out_sem, 16)
            sp.wait_ge(out_sem, 16 * MT)

        @block.gpsimd
        def _(pool):
            nc.gpsimd.memset(ones[:], 1.0).then_inc(pool_step, 1)
            nc.gpsimd.memset(epst[:], EPS).then_inc(pool_step, 1)
            pool.wait_ge(pool_step, 2)
            nc.gpsimd.affine_select(out=ident[:], in_=ones[:], compare_op=ALU.is_equal, fill=0.0,
                                    base=0, pattern=[[-1, P]], channel_multiplier=1).then_inc(pool_const, 1)
            nc.gpsimd.affine_select(out=tri[:], in_=ones[:], compare_op=ALU.is_gt, fill=0.0,
                                    base=0, pattern=[[1, P]], channel_multiplier=-1).then_inc(pool_const, 1)
            nc.gpsimd.iota(iota[:], [[1, T]], base=0, channel_multiplier=0,
                           allow_small_or_imprecise_dtypes=True).then_inc(pool_const, 1)
            nc.gpsimd.iota(dist[:, 0:P], [[-1, P]], base=0, channel_multiplier=1,
                           allow_small_or_imprecise_dtypes=True).then_inc(pool_step, 1)
            nc.gpsimd.iota(dist[:, P:3 * P], [[-1, T]], base=P, channel_multiplier=1,
                           allow_small_or_imprecise_dtypes=True).then_inc(pool_step, 1)
            pool.wait_ge(pool_step, 4)
            nc.gpsimd.affine_select(out=dist[:, 0:P], in_=dist[:, 0:P], compare_op=ALU.is_ge, fill=FAR,
                                    base=0, pattern=[[-1, P]], channel_multiplier=1).then_inc(pool_const, 1)
            nc.gpsimd.affine_select(out=dist[:, P:3 * P], in_=dist[:, P:3 * P], compare_op=ALU.is_ge, fill=FAR,
                                    base=P, pattern=[[-1, T]], channel_multiplier=1).then_inc(pool_const, 1)
            nc.gpsimd.memset(hp, 0.0).then_inc(pool_const, 1)
            pool.wait_ge(rqk_ready, 1)
            pool.wait_ge(q_copied, 4)
            for i, t in enumerate((qn, kn)):
                v = t.rearrange("p m (h d) -> p (m h) d", d=HD)
                f = rqk[:, i * 16:i * 16 + 16].unsqueeze(2).to_broadcast([P, 16, HD])
                nc.gpsimd.tensor_tensor(v, v, f, ALU.mult).then_inc(pool_qk, 1)
            for h in range(HEADS):
                pool.wait_ge(rsm_ready, h + 1)
                s = sc[h % 2]
                nc.gpsimd.tensor_scalar(s[:, 0:P], s[:, 0:P], rsm[:, h % 2, 0:1], None, ALU.mult).then_inc(pool_p, 1)
                nc.gpsimd.tensor_scalar(s[:, P:3 * P], s[:, P:3 * P], rsm[:, h % 2, 1:2], None, ALU.mult).then_inc(pool_p, 1)

        @block.scalar
        def _(act):
            steps = [0]

            def step(ins):
                steps[0] += 1
                ins.then_inc(act_step, 1)
                act.wait_ge(act_step, steps[0])

            r = 0
            for src, n in ((norm1_g, 8), (norm2_g, 8), (b_gates, 16), (conv_dw_b, 4), (conv_ln_g, 4), (conv_ln_b, 4)):
                act.dma_start(rows[r:r + n, :], src.rearrange("(r c) -> r c", c=P)).then_inc(par_in, 16)
                r += n
            for src in (q_norm_g, k_norm_g):
                for half in range(2):
                    act.dma_start(rows[r:r + 1, half * HD:(half + 1) * HD], src.rearrange("(r c) -> r c", r=1)).then_inc(par_in, 16)
                r += 1
            act.dma_start(dwr, conv_dw).then_inc(par_in, 16)
            act.dma_start(brt[:], b_router.partition_broadcast(P)).then_inc(small_in, 16)
            act.dma_start(wr[:], w_router.rearrange("(k p) n -> p k n", p=P)).then_inc(small_in, 16)
            act.dma_start(bdown[:], b_down).then_inc(small_in, 16)

            act.wait_ge(x_in, 16)
            act.wait_ge(pool_const, 1)
            for m in range(MT):
                step(nc.scalar.activation(junk, hx[:, m, :], ACT.Square, accum_out=st[:, m:m + 1]))
            nc.scalar.activation(st[:, 2:4], st[:, 0:2], ACT.Sqrt, bias=epst[:], scale=1.0 / D).then_inc(ssx, 1)

            for b in range(2):
                u = U_G + b
                full(act, u)
                nc.scalar.activation(aT[:, 2 * b:2 * b + 2, :], bank[u % 4][:].rearrange("p (a b) -> p a b", a=2),
                                     ACT.Identity).then_inc(bank_free[u % 4], 1)
            for b in range(2):
                u = U_G + 2 + b
                full(act, u)
                nc.scalar.activation(sq[:, 2 * b:2 * b + 2, :], bank[u % 4][:].rearrange("p (a b) -> p a b", a=2),
                                     ACT.Sigmoid).then_inc(bank_free[u % 4], 1)
            for i, t in enumerate((qn, kn)):
                for m in range(MT):
                    u = U_G + 4 + 2 * i + m
                    full(act, u)
                    nc.scalar.activation(t[:, m, :], bank[u % 4][:], ACT.Identity).then_inc(q_copied, 1)
                    for h in range(HEADS):
                        c = i * 16 + m * 8 + h
                        o = m * 512 + h * HD
                        ins = nc.scalar.activation(junk[:, o:o + HD], bank[u % 4][:, h * HD:(h + 1) * HD],
                                                   ACT.Square, accum_out=ssqk[:, c:c + 1])
                    ins.then_inc(bank_free[u % 4], 1)
                    freed(act, u)
            nc.scalar.activation(rqk[:], ssqk[:], ACT.Sqrt, bias=epst[:], scale=1.0 / HD).then_inc(qk_std, 1)
            for m in range(MT):
                u = U_G + 8 + m
                full(act, u)
                nc.scalar.activation(vv[:, m, :], bank[u % 4][:], ACT.Identity).then_inc(bank_free[u % 4], 1)

            for i in range(17):
                if i % 2 == 1 and i < 16:
                    b = (i - 1) // 2
                    u = U_G + 10 + b
                    full(act, u)
                    for c in range(2):
                        k = 2 * b + c
                        ins = nc.scalar.activation(gates[:, k, :], bank[u % 4][:, c * T:(c + 1) * T], ACT.Identity,
                                                   bias=bgc[:, k:k + 1])
                    ins.then_inc(bank_free[u % 4], 1)
                h = i - 3
                if 0 <= h < HEADS:
                    act.wait_ge(nmx_ready, h + 1)
                    s = sc[h % 2]
                    nc.scalar.activation(s[:, 0:P], s[:, 0:P], ACT.Exp, bias=nmx[:, h % 2, 0:1], scale=HD ** -0.5,
                                         accum_out=sm[:, h % 2, 0:1]).then_inc(exp_done, 1)
                    nc.scalar.activation(s[:, P:3 * P], s[:, P:3 * P], ACT.Exp, bias=nmx[:, h % 2, 1:2], scale=HD ** -0.5,
                                         accum_out=sm[:, h % 2, 1:2]).then_inc(exp_done, 1)
                h = i - 4
                if 0 <= h < HEADS:
                    act.wait_ge(t_full, h + 1)
                    if h >= 2:
                        act.wait_ge(pv_done, h - 1)
                    nc.scalar.activation(pT[h % 2], T_BANK[:, 0:384].rearrange("p (a b) -> p a b", a=3),
                                         ACT.Identity).then_inc(t_read, 1)
                if i >= 7 and i % 2 == 1 and (i - 7) // 2 < KC:
                    c = (i - 7) // 2
                    act.wait_ge(pv_done, 2 * c + 2)
                    nc.scalar.activation(aoT[:, c, :], O_BANK[:, 0:T], ACT.Identity).then_inc(o_read, 1)
            for b in range(8):
                freed(act, U_G + 10 + b)
            nc.scalar.activation(gates, gates, ACT.Sigmoid).then_inc(gates_ready, 1)

            freed(act, U_MEAN)
            nc.scalar.activation(sq, xc, ACT.Square).then_inc(sqr_ready, 1)
            full(act, U_VAR)
            nc.scalar.activation(std_c, bank[U_VAR % 4][:, 0:T], ACT.Sqrt, bias=epst[:], scale=1.0 / CC).then_inc(bank_free[U_VAR % 4], 1)
            act.wait_ge(z_ready, 1)
            nc.scalar.activation(sq, xc, ACT.Sigmoid).then_inc(sig_ready, 1)

            for j in range(4):
                n, m = divmod(j, 2)
                freed(act, U_OUT + j)
                step(nc.scalar.activation(junk2, hx[:, m, n * 512:(n + 1) * 512], ACT.Square,
                                          accum_out=st[:, 8 + 2 * m + n:9 + 2 * m + n]))
            for m in range(MT):
                step(nc.scalar.activation(st[:, 12 + m:13 + m], st[:, 8 + 2 * m:9 + 2 * m], ACT.Identity, bias=st[:, 9 + 2 * m:10 + 2 * m]))
            nc.scalar.activation(st[:, 14:16], st[:, 12:14], ACT.Sqrt, bias=epst[:], scale=1.0 / D).then_inc(std2, 1)
            for m in range(MT):
                act.wait_ge(v0_ready, m + 1)
                nc.scalar.activation(gt4[:, m, :], top[:, m, 0:TOPK], ACT.Exp, bias=st[:, 16 + m:17 + m],
                                     accum_out=st[:, 18 + m:19 + m]).then_inc(expg, 1)

            act.wait_ge(cum_ready, 1)
            items = act.value_load(cum[0:1, E:E + 1], min_val=1, max_val=63)
            with act.Fori(0, items) as n:
                act.wait_ge(clip_ready, n + 1)
                nc.scalar.activation(ACT_B, ACT_A, ACT.Sigmoid, scale=ALPHA).then_inc(sigm_ready, 1)
                act.wait_ge(actT_full, n + 1)
                nc.scalar.activation(actT, GA[:].rearrange("p (i s) -> p i s", i=4), ACT.Identity).then_inc(actT_ready, 1)
                act.wait_ge(down_done, 4 * n + 4)
                nc.scalar.activation(YS, YB[:], ACT.Identity).then_inc(y_ready, 1)
            act.wait_ge(scattered, items + 1)
            for m in range(MT):
                nc.scalar.activation(outs[:, m, 0:512], acc[2 * m][:], ACT.Identity).then_inc(out_left, 1)

        @block.vector
        def _(dve):
            steps = [0]

            def done(ins):
                steps[0] += 1
                ins.then_inc(dve_step, 1)
                return steps[0]

            def step(ins):
                dve.wait_ge(dve_step, done(ins))

            full(dve, U_PAR)
            step(nc.vector.tensor_copy(par[:], bank[0][:, 0:46]))
            nc.vector.tensor_copy(dwT[:], bank[0][:, 64:64 + KC * TAPS].rearrange("p (c w) -> p c w", c=KC)).then_inc(bank_free[0], 1)
            dve.wait_ge(ssx, 1)
            step(nc.vector.reciprocal(st[:, 4:6], st[:, 2:4]))
            for m in range(MT):
                nc.vector.tensor_scalar(xn[:, m, :], hx[:, m, :], st[:, 4 + m:5 + m], None, ALU.mult).then_inc(xn_ready, 1)
            for m in range(MT):
                for b in range(2):
                    u = U_XT + 2 * m + b
                    full(dve, u)
                    nc.vector.tensor_tensor(uT[:, 4 * b:4 * b + 4, m * P:(m + 1) * P],
                                            bank[u % 4][:].rearrange("p (a b) -> p a b", a=4),
                                            g1c[:, 4 * b:4 * b + 4].unsqueeze(2).to_broadcast([P, 4, P]),
                                            ALU.mult).then_inc(bank_free[u % 4], 1)

            dve.wait_ge(pool_const, 6)
            for b in range(2):
                for u in (U_G + b, U_G + 2 + b):
                    freed(dve, u)
                nc.vector.tensor_tensor(hp[:, 2 * b:2 * b + 2, TAPS - 1:], aT[:, 2 * b:2 * b + 2, :],
                                        sq[:, 2 * b:2 * b + 2, :], ALU.mult).then_inc(a_ready, 1)
            dve.wait_ge(a_ready, 2)
            landed = [0] * KC
            for w in range(TAPS):
                for c in range(KC):
                    tap = hp[:, c, w:w + T]
                    if w == 0:
                        landed[c] = done(nc.vector.tensor_scalar(cv[:, c, :], tap, dwT[:, c, 0:1], dwb[:, c:c + 1], ALU.mult, ALU.add))
                    else:
                        dve.wait_ge(dve_step, landed[c])
                        ins = nc.vector.scalar_tensor_tensor(cv[:, c, :], tap, dwT[:, c, w:w + 1], cv[:, c, :], ALU.mult, ALU.add)
                        if w == TAPS - 1 and c == KC - 1:
                            ins.then_inc(cv_done, 1)
                        else:
                            landed[c] = done(ins)
                if w == 24:
                    dve.wait_ge(qk_std, 1)
                    nc.vector.reciprocal(rqk[:], rqk[:]).then_inc(rqk_ready, 1)

            for j in range(4):
                i, m = divmod(j, 2)
                dve.wait_ge(qkT_full, j + 1)
                nc.vector.tensor_scalar((qT, kT)[i][:, :, m * P:(m + 1) * P], bank[4 + j][:].rearrange("p (a b) -> p a b", a=4),
                                        (qg, kg)[i], None, ALU.mult).then_inc(qkT_ready, 1)
            for h in range(HEADS + 1):
                if h < HEADS:
                    s = sc[h % 2]
                    slope = 2.0 ** (-8.0 * (h + 1) / HEADS)
                    dve.wait_ge(s_full, h + 1)
                    if h >= 2:
                        dve.wait_ge(t_full, h - 1)
                    nc.vector.scalar_tensor_tensor(s, dist, -slope * HD ** 0.5, S_BANKS[h % 2][:, 0:384],
                                                   ALU.mult, ALU.add).then_inc(s_read, 1)
                    dve.wait_ge(s_read, h + 1)
                    done(nc.vector.reduce_max(mx[:, h % 2, 0:1], s[:, 0:P], AX.X))
                    step(nc.vector.reduce_max(mx[:, h % 2, 1:2], s[:, P:3 * P], AX.X))
                    nc.vector.tensor_scalar(nmx[:, h % 2, :], mx[:, h % 2, :], -HD ** -0.5, None, ALU.mult).then_inc(nmx_ready, 1)
                if h >= 1:
                    dve.wait_ge(exp_done, 2 * h)
                    nc.vector.reciprocal(rsm[:, (h - 1) % 2, :], sm[:, (h - 1) % 2, :]).then_inc(rsm_ready, 1)

            full(dve, U_MEAN)
            dve.wait_ge(cv_done, 1)
            nc.vector.scalar_tensor_tensor(xc, bank[U_MEAN % 4][:, 0:T].unsqueeze(1).to_broadcast([P, KC, T]), -1.0 / CC, cv,
                                           ALU.mult, ALU.add).then_inc(bank_free[U_MEAN % 4], 1)

            def gated_attention(b):
                u = U_ATT + b
                full(dve, u)
                dve.wait_ge(gates_ready, 1)
                nc.vector.tensor_tensor(mixT[:, 2 * b:2 * b + 2, :], bank[u % 4][:].rearrange("p (a b) -> p a b", a=2),
                                        gates[:, 8 + 2 * b:10 + 2 * b, :], ALU.mult).then_inc(bank_free[u % 4], 1)

            for b in range(2):
                gated_attention(b)
            freed(dve, U_VAR)
            step(nc.vector.reciprocal(rstd_c, std_c))
            step(nc.vector.tensor_tensor(xc, xc, rstd_c.unsqueeze(1).to_broadcast([P, KC, T]), ALU.mult))
            for c in range(KC):
                ins = nc.vector.tensor_scalar(xc[:, c, :], xc[:, c, :], lng[:, c:c + 1], lnb[:, c:c + 1], ALU.mult, ALU.add)
            ins.then_inc(z_ready, 1)
            dve.wait_ge(z_ready, 1)
            dve.wait_ge(sig_ready, 1)
            nc.vector.tensor_tensor(cv, xc, sq, ALU.mult).then_inc(cT_ready, 1)
            for b in range(2, 4):
                gated_attention(b)
            for b in range(4):
                u = U_CONV + b
                full(dve, u)
                if b >= 1:
                    dve.wait_ge(mix_ready, b)
                nc.vector.tensor_tensor(prod, bank[u % 4][:].rearrange("p (a b) -> p a b", a=2),
                                        gates[:, 2 * b:2 * b + 2, :], ALU.mult).then_inc(bank_free[u % 4], 1)
                freed(dve, u)
                freed(dve, U_ATT + b)
                nc.vector.tensor_tensor(mixT[:, 2 * b:2 * b + 2, :], mixT[:, 2 * b:2 * b + 2, :], prod, ALU.add).then_inc(mix_ready, 1)
            for j in range(4):
                n, m = divmod(j, 2)
                u = U_OUT + j
                full(dve, u)
                hs = hx[:, m, n * 512:(n + 1) * 512]
                nc.vector.tensor_tensor(hs, hs, bank[u % 4][:], ALU.add).then_inc(bank_free[u % 4], 1)
            dve.wait_ge(std2, 1)
            step(nc.vector.reciprocal(st[:, 6:8], st[:, 14:16]))
            used(dve, OUT_W + 1)
            for m in range(MT):
                nc.vector.tensor_scalar(u2[:, m, :], hx[:, m, :], st[:, 6 + m:7 + m], None, ALU.mult).then_inc(u2_ready, 1)
            for j in range(4):
                m, b = divmod(j, 2)
                u = U_U2T + j
                full(dve, u)
                nc.vector.tensor_tensor(u2T[:, 4 * b:4 * b + 4, m * P:(m + 1) * P],
                                        bank[u % 4][:].rearrange("p (a b) -> p a b", a=4),
                                        g2c[:, 4 * b:4 * b + 4].unsqueeze(2).to_broadcast([P, 4, P]),
                                        ALU.mult).then_inc(bank_free[u % 4], 1)
            full(dve, U_LOG)
            dve.wait_ge(small_in, 48)
            nc.vector.tensor_tensor(lg[:], bank[U_LOG % 4][:, 0:MT * E].rearrange("p (m e) -> p m e", m=MT),
                                    brt[:].unsqueeze(1).to_broadcast([P, MT, E]), ALU.add).then_inc(bank_free[U_LOG % 4], 1)
            freed(dve, U_LOG)
            for m in range(MT):
                step(nc.vector.max(top[:, m, :], lg[:, m, :]))
                nc.vector.tensor_scalar(st[:, 16 + m:17 + m], top[:, m, 0:1], -1.0, None, ALU.mult).then_inc(v0_ready, 1)
                step(nc.vector.max_index(topi[:, m, :], top[:, m, :], lg[:, m, :]))
            step(nc.vector.tensor_copy(topf[:], topi[:]))
            for m in range(MT):
                step(nc.vector.tensor_tensor(eq, iota[:, 0:E].unsqueeze(1).to_broadcast([P, TOPK, E]),
                                             topf[:, m, 0:TOPK].unsqueeze(2).to_broadcast([P, TOPK, E]), ALU.is_equal))
                nc.vector.tensor_reduce(msk[:, m, :], eq.rearrange("p j e -> p e j"), AX.X, ALU.add).then_inc(tab_ready, 1)
                dve.wait_ge(expg, m + 1)
                step(nc.vector.reciprocal(st[:, 18 + m:19 + m], st[:, 18 + m:19 + m]))
                step(nc.vector.tensor_scalar(gt4[:, m, :], gt4[:, m, :], st[:, 18 + m:19 + m], None, ALU.mult))
                dve.wait_ge(tab_ready, m + 1)
                step(nc.vector.tensor_tensor(eq, eq, gt4[:, m, :].unsqueeze(2).to_broadcast([P, TOPK, E]), ALU.mult))
                nc.vector.tensor_reduce(gate[:, m, :], eq.rearrange("p j e -> p e j"), AX.X, ALU.add).then_inc(gTf, 1)
                dve.wait_ge(gTf, m + 1)
            full(dve, U_TAB)
            tb = bank[U_TAB % 4]
            step(nc.vector.scalar_tensor_tensor(pos[:], tb[:, 0:2 * E].rearrange("p (m e) -> p m e", m=MT), 1.0, msk[:], ALU.add, ALU.mult))
            done(nc.vector.tensor_scalar(pos[:], pos[:], -1.0, None, ALU.add))
            step(nc.vector.tensor_scalar(cnt[0:1, 0, :], tb[0:1, 2 * E:3 * E], float(SLOTS), 1.0, ALU.is_gt, ALU.add))
            step(nc.vector.tensor_scalar(cnt[0:1, 1, :], tb[0:1, 2 * E:3 * E], 2.0 * SLOTS, None, ALU.is_gt))
            step(nc.vector.tensor_tensor(cnt[0:1, 0, :], cnt[0:1, 0, :], cnt[0:1, 1, :], ALU.add))
            nc.vector.tensor_scalar(cnt[0:1, 1, :], tb[0:1, 2 * E:3 * E], 3.0 * SLOTS, None, ALU.is_gt).then_inc(bank_free[U_TAB % 4], 1)
            freed(dve, U_TAB)
            step(nc.vector.tensor_tensor(cnt[0:1, 0, :], cnt[0:1, 0, :], cnt[0:1, 1, :], ALU.add))
            done(nc.vector.memset(cumf, 0.0))
            step(nc.vector.memset(cnt[0:1, 2, :], 1.0))
            step(nc.vector.tensor_tensor_scan(cumf[0:1, 1:E + 1], cnt[0:1, 2, :], cnt[0:1, 0, :], 0.0, ALU.mult, ALU.add))
            step(nc.vector.tensor_scalar(cumf[0:1, E + 1:2 * E + 1], cumf[0:1, 1:E + 1], -1.0, None, ALU.add))
            nc.vector.tensor_copy(cum[:], cumf).then_inc(cum_ready, 1)
            full(dve, U_GT)
            dve.wait_ge(seeded, 1)
            nc.vector.tensor_copy(gT, bank[U_GT % 4][0:E, 0:T]).then_inc(gT_ready, 1)
            nc.vector.memset(YS, 0.0).then_inc(y_ready, 1)
            dve.wait_ge(cum_ready, 1)
            nc.vector.memset(hotT, 0.0).then_inc(hotT_ready, 1)
            nc.vector.memset(ACT_C, 0.0).then_inc(h_free, 1)

            with dve.Fori(0, E) as e:
                first = dve.value_load(cum[0:1, bass.ds(e, 1)], min_val=0, max_val=62)
                end = dve.value_load(cum[0:1, bass.ds(e + 1, 1)], min_val=1, max_val=63)
                with dve.Fori(first, end) as n:
                    base = nc.s_assert_within((n - first) * SLOTS, 0, T - SLOTS, skip_runtime_bounds_check_because="an expert has at most T tokens, so MAX_TILES items")
                    for m in range(MT):
                        nc.vector.tensor_scalar(hot[:, m, :], iota[:, bass.ds(base, SLOTS)], pos[:, m, bass.ds(e, 1)], None,
                                                ALU.is_equal).then_inc(hot_ready, 1)
                        nc.vector.tensor_scalar(hotg[:, m, :].rearrange("p (r s) -> p r s", r=2),
                                                iota[:, bass.ds(base, SLOTS)].unsqueeze(1).to_broadcast([P, 2, SLOTS]),
                                                pos[:, m, bass.ds(e, 1)], gate[:, m, bass.ds(e, 1)],
                                                ALU.is_equal, ALU.mult).then_inc(hot_ready, 1)
                    nc.vector.tensor_scalar(sel[:], ident[0:E, bass.ds(e, 1)].to_broadcast([E, SLOTS]), 1.0, None,
                                            ALU.mult).then_inc(hot_ready, 1)
                    dve.wait_ge(gathered, n + 1)
                    nc.vector.tensor_tensor(XT, GA[:].rearrange("p (k s) -> p k s", k=KD),
                                            g2c.unsqueeze(2).to_broadcast([P, KD, SLOTS]), ALU.mult).then_inc(xt_ready, 1)
                    dve.wait_ge(scattered, n + 1)
                    nc.vector.tensor_copy(hotT, YB[:, 0:T].rearrange("p (m t) -> p m t", m=MT)).then_inc(hotT_ready, 1)
                    dve.wait_ge(up_done, KD * n + KD)
                    nc.vector.tensor_scalar(ACT_A, HG[:], LIMIT, None, ALU.min).then_inc(clip_ready, 1)
                    nc.vector.tensor_scalar(ACT_C, HL[:], LIMIT, -LIMIT, ALU.min, ALU.max).then_inc(h_free, 1)
                    dve.wait_ge(clip_ready, n + 1)
                    dve.wait_ge(h_free, n + 2)
                    nc.vector.scalar_tensor_tensor(ACT_C, ACT_C, 1.0, ACT_A, ALU.add, ALU.mult).then_inc(moe_step, 1)
                    dve.wait_ge(moe_step, n + 1)
                    dve.wait_ge(sigm_ready, n + 1)
                    nc.vector.tensor_tensor(ACT_A, ACT_C, ACT_B, ALU.mult).then_inc(act_ready, 1)
            items = dve.value_load(cum[0:1, E:E + 1], min_val=1, max_val=63)
            dve.wait_ge(scattered, items + 1)
            for m in range(MT):
                nc.vector.tensor_copy(outs[:, m, 512:1024], acc[2 * m + 1][:]).then_inc(out_right, 1)

        @block.tensor
        def _(pe):
            mm = nc.tensor.matmul

            def claim(u):
                if u >= 4:
                    freed(pe, u - 4)

            def product(o, lhs, rhs, n):
                for k in range(n):
                    ins = mm(o, lhs(k), rhs(k), start=(k == 0), stop=(k == n - 1))
                return ins

            pe.wait_ge(pool_const, 1)
            pe.wait_ge(par_in, 16 * 11)
            nc.tensor.transpose(bank[0][:, 0:46], rows, ident[0:46, 0:46])
            for c in range(KC):
                ins = nc.tensor.transpose(bank[0][:, 64 + c * TAPS:64 + (c + 1) * TAPS], dwr[:, c * P:(c + 1) * P], ident[0:TAPS, 0:TAPS])
            ins.then_inc(bank_full[0], 1)
            for m in range(MT):
                pe.wait_ge(xn_ready, m + 1)
                for b in range(2):
                    u = U_XT + 2 * m + b
                    claim(u)
                    for j in range(4):
                        k = 4 * b + j
                        ins = nc.tensor.transpose(bank[u % 4][:, j * P:(j + 1) * P], xn[:, m, k * P:(k + 1) * P], ident[:])
                    ins.then_inc(bank_full[u % 4], 1)

            def channel_group_bank(i, b, after=None):
                w = stream[i][1]
                u = U_G + 2 * i + b
                claim(u)
                for c in range(2):
                    ch = 2 * b + c
                    ins = product(bank[u % 4][:, c * T:(c + 1) * T], lambda k: w[:, k, ch * P:(ch + 1) * P], lambda k: uT[:, k, :], KD)
                    if c == 1:
                        ins.then_inc(bank_full[u % 4], 1)
                    elif after:
                        after()
                return ins

            def arrived(i):
                pe.wait_ge(slot_in[i % 3], 16 * (i // 3 + 1))

            for b in range(4):
                freed(pe, U_XT + b)
            for i in range(2):
                arrived(i)
                for b in range(2):
                    channel_group_bank(i, b)
            for i in range(2, 5):
                arrived(i)
                w = stream[i][1]
                for m in range(MT):
                    u = U_G + 2 * i + m
                    claim(u)
                    product(bank[u % 4][:], lambda k: uT[:, k, m * P:(m + 1) * P], lambda k: w[:, k, :], KD).then_inc(bank_full[u % 4], 1)

            def head(h):
                q0 = (h % 2) * HD
                return slice(q0, q0 + HD), h // 2

            def scores(h):
                r, c = head(h)
                if h < 2:
                    pe.wait_ge(qkT_ready, 4)
                else:
                    pe.wait_ge(s_read, h - 1)
                s = S_BANKS[h % 2]
                mm(s[:, 0:P], qT[r, c, 0:P], kT[r, c, 0:P], start=True, stop=True)
                mm(s[:, P:3 * P], qT[r, c, P:T], kT[r, c, :], start=True, stop=True).then_inc(s_full, 1)

            def transposed_probs(h):
                pe.wait_ge(pool_p, 2 * h + 2)
                if h >= 1:
                    pe.wait_ge(t_read, h)
                for j in range(3):
                    ins = nc.tensor.transpose(T_BANK[:, j * P:(j + 1) * P], sc[h % 2][:, j * P:(j + 1) * P], ident[:])
                ins.then_inc(t_full, 1)

            def attend(h):
                r, c = head(h)
                pe.wait_ge(t_read, h + 1)
                if h % 2 == 0 and h >= 2:
                    pe.wait_ge(o_read, h // 2)
                p = pT[h % 2]
                v = [vv[:, m, h * HD:(h + 1) * HD] for m in range(MT)]
                mm(O_BANK[r, 0:P], v[0], p[:, 0, :], start=True, stop=True)
                mm(O_BANK[r, P:T], v[0], p[:, 1, :], start=True, stop=False)
                mm(O_BANK[r, P:T], v[1], p[:, 2, :], start=False, stop=True).then_inc(pv_done, 1)

            def qk_transposes():
                pe.wait_ge(pool_qk, 2)
                for j in range(4):
                    i, m = divmod(j, 2)
                    for c in range(KC):
                        ins = nc.tensor.transpose(bank[4 + j][:, c * P:(c + 1) * P], (qn, kn)[i][:, m, c * P:(c + 1) * P], ident[:])
                    ins.then_inc(qkT_full, 1)

            def between(i):
                if i == 1:
                    qk_transposes()
                if 0 <= i - 2 < HEADS:
                    scores(i - 2)
                if 0 <= i - 4 < HEADS:
                    transposed_probs(i - 4)
                if 0 <= i - 5 < HEADS:
                    if i == 5:
                        freed(pe, U_G + 8)
                        freed(pe, U_G + 9)
                    attend(i - 5)

            for i in range(5, GROUPS):
                arrived(i)
                for b in range(2):
                    slot = 4 * (i - 5) + 2 * b
                    channel_group_bank(i, b, lambda: between(slot))
                    between(slot + 1)

            pe.wait_ge(cv_done, 1)
            claim(U_MEAN)
            product(bank[U_MEAN % 4][:, 0:T], lambda k: ones[:], lambda k: cv[:, k, :], KC).then_inc(bank_full[U_MEAN % 4], 1)

            def branch(i, base, src, b):
                w = stream[i][1]
                u = base + b
                claim(u)
                for c in range(2):
                    ch = 2 * b + c
                    ins = product(bank[u % 4][:, c * T:(c + 1) * T], lambda k: w[:, k, ch * P:(ch + 1) * P], lambda k: src[:, k, :], KC)
                ins.then_inc(bank_full[u % 4], 1)

            arrived(ATT_W)
            pe.wait_ge(o_read, KC)
            for b in range(4):
                branch(ATT_W, U_ATT, aoT, b)
            claim(U_VAR)
            pe.wait_ge(sqr_ready, 1)
            product(bank[U_VAR % 4][:, 0:T], lambda k: ones[:], lambda k: sq[:, k, :], KC).then_inc(bank_full[U_VAR % 4], 1)
            arrived(CONV_W)
            pe.wait_ge(cT_ready, 1)
            for b in range(4):
                branch(CONV_W, U_CONV, cv, b)
            pe.wait_ge(mix_ready, 4)
            for n in range(2):
                arrived(OUT_W + n)
                w = stream[OUT_W + n][1]
                for m in range(MT):
                    u = U_OUT + 2 * n + m
                    claim(u)
                    product(bank[u % 4][:], lambda k: mixT[:, k, m * P:(m + 1) * P], lambda k: w[:, k, :], KD).then_inc(bank_full[u % 4], 1)
            for j in range(4):
                freed(pe, U_OUT + j)
            for m in range(MT):
                for n in range(2):
                    ins = mm(acc[2 * m + n][:], ident[:], hx[:, m, n * 512:(n + 1) * 512], start=True, stop=False, skip_group_check=True)
            ins.then_inc(seeded, 1)
            for m in range(MT):
                pe.wait_ge(u2_ready, m + 1)
                for b in range(2):
                    u = U_U2T + 2 * m + b
                    claim(u)
                    for j in range(4):
                        k = 4 * b + j
                        ins = nc.tensor.transpose(bank[u % 4][:, j * P:(j + 1) * P], u2[:, m, k * P:(k + 1) * P], ident[:])
                    ins.then_inc(bank_full[u % 4], 1)
            for b in range(4):
                freed(pe, U_U2T + b)
            pe.wait_ge(small_in, 48)
            claim(U_LOG)
            for m in range(MT):
                ins = product(bank[U_LOG % 4][:, m * E:(m + 1) * E], lambda k: u2T[:, k, m * P:(m + 1) * P], lambda k: wr[:, k, :], KD)
            ins.then_inc(bank_full[U_LOG % 4], 1)
            pe.wait_ge(tab_ready, MT)
            claim(U_TAB)
            tb = bank[U_TAB % 4]
            mm(tb[:, 0:E], tri[:], msk[:, 0, :], start=True, stop=True)
            mm(tb[:, E:2 * E], ones[:], msk[:, 0, :], start=True, stop=False)
            mm(tb[:, E:2 * E], tri[:], msk[:, 1, :], start=False, stop=True)
            mm(tb[:, 2 * E:3 * E], ones[:], msk[:, 0, :], start=True, stop=False)
            mm(tb[:, 2 * E:3 * E], ones[:], msk[:, 1, :], start=False, stop=True).then_inc(bank_full[U_TAB % 4], 1)
            pe.wait_ge(gTf, MT)
            claim(U_GT)
            for m in range(MT):
                ins = mm(bank[U_GT % 4][0:E, m * P:(m + 1) * P], gate[:, m, :], ident[:], start=True, stop=True)
            ins.then_inc(bank_full[U_GT % 4], 1)
            pe.wait_ge(gT_ready, 1)
            for m in range(MT):
                for n in range(2):
                    mm(acc[2 * m + n][:], gT[:, m * P:(m + 1) * P], bdown[:, n * 512:(n + 1) * 512],
                       start=False, stop=False, skip_group_check=True)

            def scatter():
                for m in range(MT):
                    for half in range(2):
                        r = slice(half * SLOTS, (half + 1) * SLOTS)
                        ins = mm(acc[2 * m + half][:], hotT[r, m, :], YS[r, :], start=False, stop=False, skip_group_check=True)
                ins.then_inc(scattered, 1)

            pe.wait_ge(bup_in, 16)
            pe.wait_ge(cum_ready, 1)
            freed(pe, U_LOG)
            with pe.Fori(0, E // 2) as pair:
                for a in range(2):
                    e = pe.snap(2 * pair + a)
                    first = pe.value_load(cum[0:1, bass.ds(e, 1)], min_val=0, max_val=62)
                    end = pe.value_load(cum[0:1, bass.ds(e + 1, 1)], min_val=1, max_val=63)
                    with pe.Fori(first, end) as n:
                        pe.wait_ge(hot_ready, 5 * n + 5)
                        for k in range(KD):
                            for m in range(MT):
                                ins = mm(GA[:, k * SLOTS:(k + 1) * SLOTS], u2[:, m, k * P:(k + 1) * P], hot[:, m, :],
                                         start=(m == 0), stop=(m == MT - 1))
                        ins.then_inc(gathered, 1)
                        pe.wait_ge(y_ready, n + 1)
                        for m in range(MT):
                            ins = nc.tensor.transpose(YB[:, m * P:(m + 1) * P], hotg[:, m, :], ident[:])
                        ins.then_inc(hotT_full, 1)
                        pe.wait_ge(hotT_ready, n + 1)
                        scatter()
                        pe.wait_ge(xt_ready, n + 1)
                        pe.wait_ge(h_free, n + 1)
                        places = [(b_[half * SLOTS:(half + 1) * SLOTS, :], (2 * g + half) * 512)
                                  for g, b_ in enumerate((HG, HL)) for half in range(2)]
                        for o, f in places:
                            mm(o, sel[:], bup[:, f:f + 512], start=True, stop=False, skip_group_check=True)
                        for k in range(KD):
                            pe.wait_ge(up_in[a][k], 16 * pair + 16)
                            for o, f in places:
                                ins = mm(o, XT[:, k, :], up[a][:, k, f:f + 512], start=False, stop=(k == KD - 1), skip_group_check=True)
                            ins.then_inc(up_done, 1)
                        pe.wait_ge(act_ready, n + 1)
                        for i in range(4):
                            ins = nc.tensor.transpose(GA[:, i * P:(i + 1) * P], ACT_A[:, i * P:(i + 1) * P], ident[:])
                        ins.then_inc(actT_full, 1)
                        pe.wait_ge(actT_ready, n + 1)
                        pe.wait_ge(hotT_ready, n + 2)
                        for c in range(4):
                            pe.wait_ge(down_in[c], 16 * e + 16)
                            for k in (2 * c, 2 * c + 1):
                                for half in range(2):
                                    ins = mm(YB[half * SLOTS:(half + 1) * SLOTS, :], actT[:, k % 4, (k // 4) * SLOTS:(k // 4 + 1) * SLOTS],
                                             down[:, k, half * 512:(half + 1) * 512], start=(k == 0), stop=(k == KD - 1), skip_group_check=True)
                            ins.then_inc(down_done, 1)
            items = pe.value_load(cum[0:1, E:E + 1], min_val=1, max_val=63)
            pe.wait_ge(y_ready, items + 1)
            pe.wait_ge(hotT_ready, items + 1)
            scatter()


_INS = ["x", "norm1_g", "w_in", "b_gates", "conv_dw", "conv_dw_b", "conv_ln_g", "conv_ln_b", "w_conv_out",
        "q_norm_g", "k_norm_g", "w_attn_out", "w_out", "norm2_g", "w_router", "b_router",
        "w_up_gate", "b_up_gate", "w_down", "b_down"]


def kernel(**inputs):
    import numpy as np
    import concourse.bacc as bacc
    from concourse.bass_utils import run_bass_kernel_spmd

    nc = bacc.Bacc("TRN2", target_bir_lowering=False, num_devices=1)
    arrays, args = {}, []
    for name in _INS:
        a = np.ascontiguousarray(inputs[name])
        a = a.reshape(a.shape[1:])
        arrays["in_" + name] = a
        args.append(nc.dram_tensor("in_" + name, a.shape, mybir.dt.from_np(a.dtype), kind="ExternalInput").ap())
    result = nc.dram_tensor("out_0", (T, D), F32, kind="ExternalOutput").ap()
    hybrid_block(nc, *args, result)
    r = run_bass_kernel_spmd(nc, [arrays], core_ids=[0])
    return r.results[0]["out_0"].reshape(1, T, D)
```

```python
import concourse.bass as bass
from concourse import mybir
from contextlib import ExitStack

F32 = mybir.dt.float32
F32R = mybir.dt.float32r
I32 = mybir.dt.int32
U32 = mybir.dt.uint32
ALU = mybir.AluOpType
ACT = mybir.ActivationFunctionType
AX = mybir.AxisListType

P = 128
T = 256
MT = T // P
D = 1024
KD = D // P
CC = 512
KC = CC // P
TAPS = 31
HEADS = 8
HD = 64
E = 32
TOPK = 4
FF = 1024
LIMIT = 7.0
ALPHA = 1.702
EPS = 1e-6
SLOTS = 64
MAX_TILES = T // SLOTS
ITEMS = TOPK * T // SLOTS + E + 1
T_FIRST, T_EXPERT, T_TILE = 0, E + 1, E + 1 + ITEMS
TABLE = T_TILE + ITEMS
GROUPS = 9
FAR = 1e30


def hybrid_block(nc, x, norm1_g, w_in, b_gates, conv_dw, conv_dw_b, conv_ln_g, conv_ln_b, w_conv_out,
                 q_norm_g, k_norm_g, w_attn_out, w_out, norm2_g, w_router, b_router,
                 w_up_gate, b_up_gate, w_down, b_down, out):
    ctx = ExitStack()
    with ctx:
        def sb(name, shape, dt=F32):
            return ctx.enter_context(nc.sbuf_tensor(name, shape, dt))

        def sem(name):
            return ctx.enter_context(nc.semaphore(name))

        def sb_placed(name, columns):
            t = sb(name, [P, columns])
            return t, nc.sbuf_base - 4 * columns

        UP_EVEN, EVEN_AT = sb_placed("up_even", KD * 2 * FF)
        UP_ODD = sb("up_odd", [P, KD * 2 * FF])
        DOWN, DOWN_AT = sb_placed("down", KD * D)
        up = [r[:, :].rearrange("p (k n) -> p k n", k=KD) for r in (UP_EVEN, UP_ODD)]
        down = DOWN[:, :].rearrange("p (k n) -> p k n", k=KD)
        REG_H = sb("reg_h", [P, 2048])
        REG_U = sb("reg_u", [P, 2048])
        REG_E, E_AT = sb_placed("reg_e", 4096)
        REG_R = sb("reg_r", [P, 1152])

        slots = [REG_E[:, :], DOWN[:, 0:4096], DOWN[:, 4096:8192]]

        def part(name, at, column, n):
            return nc.alloc_sbuf_tensor_at(name, [P, n], F32R, offset=at + 4 * column)

        w_lo = [part("w_lo0", E_AT, 0, 4096), part("w_lo1", DOWN_AT, 0, 4096), part("w_lo2", DOWN_AT, 4096, 4096)]
        w_hi = [part("w_hi0", EVEN_AT, 0, 4096), part("w_hi1", EVEN_AT, 4096, 4096)]
        u_r = [part(n, EVEN_AT, 8192 + 2048 * i, 2048)[:, :].rearrange("p (k t) -> p k t", k=KD)
               for i, n in enumerate(("u_hi", "u_lo"))]
        ao_r = [part(n, EVEN_AT, 12288 + 1024 * i, 1024)[:, :].rearrange("p (k t) -> p k t", k=KC)
                for i, n in enumerate(("ao_hi", "ao_lo"))]
        cv_r = [part(n, EVEN_AT, 14336 + 1024 * i, 1024)[:, :].rearrange("p (k t) -> p k t", k=KC)
                for i, n in enumerate(("cv_hi", "cv_lo"))]

        def tmp(at, n, **kw):
            v = UP_ODD[:, at:at + n]
            return v.rearrange("p (a b) -> p a b", **kw) if kw else v

        gates = tmp(0, 4096, a=16)
        xn = tmp(0, 2048, a=MT)
        junk = tmp(2048, 1024)
        aT = tmp(4096, 1024, a=KC)
        hp = tmp(5120, KC * (T + TAPS - 1), a=KC)
        cv = tmp(6272, 1024, a=KC)
        xc = tmp(7296, 1024, a=KC)
        sq = tmp(8320, 1024, a=KC)
        qn = tmp(9344, 1024, a=MT)
        kn = tmp(10368, 1024, a=MT)
        vv = tmp(11392, 1024, a=MT)
        qT = tmp(12416, 1024, a=KC)
        kT = tmp(13440, 1024, a=KC)
        dist = tmp(14464, 384)
        pT = [tmp(14848 + 384 * i, 384, a=3) for i in range(2)]
        rstd_c = tmp(15616, 256)
        std_c = tmp(15872, 256)
        prod = sq[:, 0:2, :]

        hx = REG_H[:, :].rearrange("p (m d) -> p m d", m=MT)
        uT = REG_U[:, :].rearrange("p (k t) -> p k t", k=KD)
        mixT = uT
        u2T = uT
        u2 = REG_E[:, 0:2048].rearrange("p (m d) -> p m d", m=MT)
        bup = REG_E[:, 2048:3072]
        rows = REG_R[0:46, 512:640]
        dwr = REG_R[0:TAPS, 0:512]
        sc = [REG_R[:, 384 * i:384 * i + 384] for i in range(2)]
        junk2 = REG_R[:, 0:512]
        eq = REG_R[:, 896:1024].rearrange("p (j e) -> p j e", j=TOPK)
        trow = REG_R[0:1, 640:640 + ITEMS]
        past = REG_R[0:E, 1024:1024 + ITEMS]

        ACT_A, ACT_B, ACT_C, YR = [REG_H[:, 512 * i:512 * i + 512] for i in range(4)]
        gT = REG_H[0:E, 512:768]
        actT = REG_U[:, 0:512].rearrange("p (i s) -> p i s", i=4)
        XT = REG_R[:, 0:512].rearrange("p (k s) -> p k s", k=KD)
        hot = REG_R[:, 512:640].rearrange("p (m s) -> p m s", m=MT)
        hotg = REG_R[:, 640:896].rearrange("p (m s) -> p m s", m=MT)
        outs = UP_EVEN[:, 0:2048].rearrange("p (m d) -> p m d", m=MT)

        bdown = sb("bdown", [E, D])
        wr = sb("wr", [P, KD, E])
        ident = sb("ident", [P, P])
        tri = sb("tri", [P, P])
        ones = sb("ones", [P, P])
        iota = sb("iota", [P, T])
        par = sb("par", [P, 46])
        dwT = sb("dwT", [P, KC, TAPS])
        epst = sb("epst", [P, 1])
        st = sb("st", [P, 24])
        ssqk = sb("ssqk", [P, 2 * MT * HEADS])
        rqk = sb("rqk", [P, 2 * MT * HEADS])
        mx = sb("mx", [P, 2, 2])
        nmx = sb("nmx", [P, 2, 2])
        sm = sb("sm", [P, 2, 2])
        rsm = sb("rsm", [P, 2, 2])
        brt = sb("brt", [P, E])
        lg = sb("lg", [P, MT, E])
        top = sb("top", [P, MT, 8])
        topi = sb("topi", [P, MT, 8], U32)
        topf = sb("topf", [P, MT, 8])
        gt4 = sb("gt4", [P, MT, TOPK])
        gate = sb("gate", [P, MT, E])
        msk = sb("msk", [P, MT, E])
        pos = sb("pos", [P, MT, E])
        tcol = sb("tcol", [E, 8])
        cum = sb("cum", [1, TABLE], I32)
        pick = sb("pick", [P, E])
        half_of = sb("half_of", [P, P])
        gcur = sb("gcur", [P, MT])
        gslot = sb("gslot", [P, 1])
        bias_r = sb("bias_r", [P, 2, 512], F32R)
        sel = sb("sel", [P, P], F32R)
        ys = sb("ys", [P, 2, 512], F32R)
        hotT = sb("hotT", [P, MT, P], F32R)

        g1c, g2c = par[:, 0:8], par[:, 8:16]
        bgc, dwb, lng, lnb = par[:, 16:32], par[:, 32:36], par[:, 36:40], par[:, 40:44]
        qg, kg = par[:, 44:45], par[:, 45:46]

        bank = [ctx.enter_context(nc.psum_tensor(f"bank{i}", [P, 512], F32)) for i in range(8)]
        HG, HL, GA, YB = bank[0:4]
        S_BANKS, T_BANK, O_BANK = bank[4:6], bank[6], bank[7]
        acc = bank[4:8]

        par_in, small_in, bup_in, out_sem = [sem(n) for n in ("par_in", "small_in", "bup_in", "out_sem")]
        x_in = [sem(f"x_in{m}") for m in range(MT)]
        slot_in = [sem(f"slot_in{i}") for i in range(3)]
        g0_in = [sem(f"g0_in{c}") for c in range(4)]
        w_hi_ready, w_lo_ready = sem("w_hi_ready"), sem("w_lo_ready")
        u_hi_ready, u_lo_ready = sem("u_hi_ready"), sem("u_lo_ready")
        mix_hi, mix_lo = sem("mix_hi"), sem("mix_lo")
        cv_hi, cv_lo, o_hi = sem("cv_hi"), sem("cv_lo"), sem("o_hi")
        up_in = [[sem(f"up_in{a}_{c}") for c in range(KD)] for a in range(2)]
        down_in = [sem(f"down_in{c}") for c in range(4)]
        bank_full = [sem(f"bank_full{i}") for i in range(4)]
        bank_free = [sem(f"bank_free{i}") for i in range(4)]
        pool_const, qk_scaled, p_scaled = sem("pool_const"), sem("qk_scaled"), sem("p_scaled")
        act_step, dve_step, pool_step = sem("act_step"), sem("dve_step"), sem("pool_step")
        xn_ready, uT_ready = sem("xn_ready"), sem("uT_ready")
        qkT_full, qkT_ready = sem("qkT_full"), sem("qkT_ready")
        ssx, qk_std, rqk_ready = sem("ssx"), sem("qk_std"), sem("rqk_ready")
        a_ready, sg_ready, q_copied, v_copied = [sem(n) for n in ("a_ready", "sg_ready", "q_copied", "v_copied")]
        s_full, s_read, t_full, t_read, o_full, o_read = [sem(n) for n in ("s_full", "s_read", "t_full", "t_read", "o_full", "o_read")]
        nmx_ready, exp_done, rsm_ready, pv_done = [sem(n) for n in ("nmx_ready", "exp_done", "rsm_ready", "pv_done")]
        cv_done, xc_ready, sqr_ready, std_ready, z_ready, sig_ready, cT_ready = [
            sem(n) for n in ("cv_done", "xc_ready", "sqr_ready", "std_ready", "z_ready", "sig_ready", "cT_ready")]
        gates_pre, gates_ready, mix_ready = [sem(n) for n in ("gates_pre", "gates_ready", "mix_ready")]
        ss2, std2, u2_ready, u2T_ready, v0_ready, expg, tab_ready, gTf, gT_ready, cum_ready = [
            sem(n) for n in ("ss2", "std2", "u2_ready", "u2T_ready", "v0_ready", "expg", "tab_ready", "gTf", "gT_ready", "cum_ready")]
        seeded = sem("seeded")
        bias_hi, bias_ready, cnt_ready, tiles_ready, ends_ready, past_ready = [
            sem(n) for n in ("bias_hi", "bias_ready", "cnt_ready", "tiles_ready", "ends_ready", "past_ready")]
        hot_ready, gathered, xt_ready, hotT_full, scattered, hotT_ready = [
            sem(n) for n in ("hot_ready", "gathered", "xt_ready", "hotT_full", "scattered", "hotT_ready")]
        up_done = [sem(f"up_done{c}") for c in range(KD)]
        down_done = [sem(f"down_done{c}") for c in range(4)]
        h_free, clip_ready, sigm_ready, act_ready, actT_full, actT_ready, y_high, y_ready, moe_step = [
            sem(n) for n in ("h_free", "clip_ready", "sigm_ready", "act_ready", "actT_full",
                             "actT_ready", "y_high", "y_ready", "moe_step")]
        out_left, out_right = sem("out_left"), sem("out_right")

        block = ctx.enter_context(nc.Block())

        win = w_in.rearrange("(k p) n -> p k n", p=P)
        stream = [(win[:, :, 512 * i:512 * i + 512], slots[i % 3].rearrange("p (k n) -> p k n", k=KD))
                  for i in range(GROUPS)]
        ATT_W, CONV_W, OUT_W = GROUPS, GROUPS + 1, GROUPS + 2
        stream.append((w_attn_out.rearrange("(k p) n -> p k n", p=P),
                       slots[ATT_W % 3].rearrange("p (k n) -> p k n", k=KC)))
        stream.append((w_conv_out.rearrange("(k p) n -> p k n", p=P),
                       slots[CONV_W % 3].rearrange("p (k n) -> p k n", k=KC)))
        wout = w_out.rearrange("(k p) n -> p k n", p=P)
        for half in range(2):
            stream.append((wout[:, :, 512 * half:512 * half + 512],
                           slots[(OUT_W + half) % 3].rearrange("p (k n) -> p k n", k=KD)))

        def w_parts(i):
            k = stream[i][1].shape[1]
            return [t[:, :].rearrange("p (k n) -> p k n", k=k) for t in (w_hi[i % 2], w_lo[i % 3])]

        def half_cols(w, b):
            n = w.shape[2] // 2
            return w[:, :, b * n:(b + 1) * n]

        def arrived(eng, i):
            eng.wait_ge(slot_in[i % 3], 16 * (i // 3 + (1 if i % 3 else 0)))

        U_PAR = 0
        U_XT = 1
        U_G = U_XT + 4

        def group_use(i, b):
            b += 2 * i
            return U_G + b + (b > 12) + (b > 14)

        U_MEAN, U_VAR = U_G + 13, U_G + 16
        U_ATT = U_G + 2 * GROUPS + 2
        U_CONV = U_ATT + 4
        U_OUT = U_CONV + 4
        U_U2T = U_OUT + 4
        U_LOG = U_U2T + 4
        U_TAB = U_LOG + 1
        U_GT = U_TAB + 1
        U_ENDS = U_GT + 1
        U_ITEMS = U_ENDS + 1
        USES = U_GT + 1

        SCORES = 4
        EXPS = SCORES + 1
        LAST_USE = [group_use(i, 1) for i in range(GROUPS)] + [U_ATT + 3, U_CONV + 3, U_OUT + 1, U_OUT + 3]

        def full(eng, u):
            eng.wait_ge(bank_full[u % 4], u // 4 + 1)

        def freed(eng, u):
            eng.wait_ge(bank_free[u % 4], u // 4 + 1)

        def used(eng, i):
            full(eng, LAST_USE[i])

        @block.sync
        def _(sp):
            for m in range(MT):
                sp.dma_start(hx[:, m, :], x[m * P:(m + 1) * P, :]).then_inc(x_in[m], 16)
            sp.dma_start(dwr, conv_dw).then_inc(par_in, 16)
            sp.dma_start(rows[16:32, :], b_gates.rearrange("(r c) -> r c", c=P)).then_inc(par_in, 16)
            for r, src in ((44, q_norm_g), (45, k_norm_g)):
                sp.dma_start(rows[r:r + 1, :].rearrange("r (h d) -> r h d", h=2),
                             src.rearrange("(r h d) -> r h d", r=1, h=1).to_broadcast([1, 2, HD])).then_inc(par_in, 16)

            def load_up(par_, c, e):
                sp.dma_start(up[par_][:, c, :], w_up_gate[e, c * P:(c + 1) * P, :]).then_inc(up_in[par_][c], 16)

            def load_down(c, e):
                sp.dma_start(down[:, 2 * c:2 * c + 2, :],
                             w_down[e, 2 * c * P:(2 * c + 2) * P, :].rearrange("(r p) n -> p r n", p=P)
                             ).then_inc(down_in[c], 16)

            for i, (src, dst) in enumerate(stream):
                if i >= 3:
                    used(sp, i - 3)
                if i == 0:
                    for c in range(4):
                        sp.dma_start(dst[:, 2 * c:2 * c + 2, :], src[:, 2 * c:2 * c + 2, :]).then_inc(g0_in[c], 16)
                else:
                    sp.dma_start(dst, src).then_inc(slot_in[i % 3], 16)
            load_up(0, 6, 0)
            used(sp, CONV_W)
            load_up(0, 7, 0)
            load_down(0, 0)
            load_down(1, 0)
            sp.wait_ge(mix_ready, 4)
            for c in range(4):
                load_up(1, c, 1)
            used(sp, OUT_W)
            load_up(0, 2, 0)
            load_up(0, 3, 0)
            load_down(2, 0)
            load_down(3, 0)
            used(sp, OUT_W + 1)
            for c in (0, 1, 4, 5):
                load_up(0, c, 0)
            for q in range(4):
                sp.dma_start(bup[q * E:(q + 1) * E, :].rearrange("e (g f) -> e g f", g=2),
                             b_up_gate.rearrange("e (g h f) -> e g h f", g=2, h=2)[:, :, q % 2, :]).then_inc(bup_in, 16)
            for c in range(4, KD):
                load_up(1, c, 1)
            sp.wait_ge(cum_ready, 1)
            with sp.Fori(1, E // 2 - 1) as pair:
                for a in range(2):
                    e = sp.snap(2 * pair + a)
                    first1 = sp.value_load(cum[0:1, bass.ds(e + (T_FIRST - 1), 1)], min_val=1, max_val=ITEMS - 1)
                    for c in range(KD):
                        sp.wait_ge(up_done[c], first1)
                        sp.dma_start(up[a][:, c, :],
                                     w_up_gate[bass.ds(e, 1), c * P:(c + 1) * P, :].rearrange("e p n -> p (e n)")
                                     ).then_inc(up_in[a][c], 16)
                    for c in range(4):
                        sp.wait_ge(down_done[c], first1)
                        sp.dma_start(down[:, 2 * c:2 * c + 2, :],
                                     w_down[bass.ds(e - 1, 1), 2 * c * P:(2 * c + 2) * P, :].rearrange(
                                         "e (r p) n -> p (e r) n", p=P)).then_inc(down_in[c], 16)
            firsts = [sp.value_load(cum[0:1, T_FIRST + e:T_FIRST + e + 1], min_val=1, max_val=ITEMS - 1)
                      for e in range(E - 3, E)]

            def last_up(e, first):
                for c in range(KD):
                    sp.wait_ge(up_done[c], first)
                    load_up(e % 2, c, e)

            def last_down(e, first):
                for c in range(4):
                    sp.wait_ge(down_done[c], first)
                    load_down(c, e)

            last_up(E - 2, firsts[0])
            last_down(E - 3, firsts[0])
            last_down(E - 2, firsts[1])
            last_up(E - 1, firsts[1])
            last_down(E - 1, firsts[2])
            for m in range(MT):
                sp.wait_ge(out_left, m + 1)
                sp.wait_ge(out_right, m + 1)
                sp.dma_start(out[m * P:(m + 1) * P, :], outs[:, m, :]).then_inc(out_sem, 16)
            sp.wait_ge(out_sem, 16 * MT)

        @block.gpsimd
        def _(pool):
            nc.gpsimd.memset(ones[:], 1.0).then_inc(pool_step, 1)
            nc.gpsimd.memset(epst[:], EPS).then_inc(pool_step, 1)
            pool.wait_ge(pool_step, 2)
            nc.gpsimd.affine_select(out=ident[:], in_=ones[:], compare_op=ALU.is_equal, fill=0.0,
                                    base=0, pattern=[[-1, P]], channel_multiplier=1).then_inc(pool_const, 1)
            nc.gpsimd.affine_select(out=tri[:], in_=ones[:], compare_op=ALU.is_gt, fill=0.0,
                                    base=0, pattern=[[1, P]], channel_multiplier=-1).then_inc(pool_const, 1)
            nc.gpsimd.iota(iota[:], [[1, T]], base=0, channel_multiplier=0,
                           allow_small_or_imprecise_dtypes=True).then_inc(pool_const, 1)
            nc.gpsimd.iota(dist[:, 0:P], [[-1, P]], base=0, channel_multiplier=1,
                           allow_small_or_imprecise_dtypes=True).then_inc(pool_step, 1)
            nc.gpsimd.iota(dist[:, P:3 * P], [[-1, T]], base=P, channel_multiplier=1,
                           allow_small_or_imprecise_dtypes=True).then_inc(pool_step, 1)
            pool.wait_ge(pool_step, 4)
            nc.gpsimd.affine_select(out=dist[:, 0:P], in_=dist[:, 0:P], compare_op=ALU.is_ge, fill=FAR,
                                    base=0, pattern=[[-1, P]], channel_multiplier=1).then_inc(pool_const, 1)
            nc.gpsimd.affine_select(out=dist[:, P:3 * P], in_=dist[:, P:3 * P], compare_op=ALU.is_ge, fill=FAR,
                                    base=P, pattern=[[-1, T]], channel_multiplier=1).then_inc(pool_const, 1)
            nc.gpsimd.memset(hp, 0.0).then_inc(pool_const, 1)
            nc.gpsimd.memset(half_of[:], 0.0).then_inc(pool_step, 1)
            pool.wait_ge(pool_step, 5)
            for q in range(4):
                pool.wait_ge(pool_const, 6 + 2 * q)
                nc.gpsimd.tensor_copy(pick[q * E:(q + 1) * E, :], ident[0:E, 0:E]).then_inc(pool_const, 1)
                c = (q % 2) * SLOTS
                pool.wait_ge(pool_const, 7 + 2 * q)
                nc.gpsimd.memset(half_of[q * E:(q + 1) * E, c:c + SLOTS], 1.0).then_inc(pool_const, 1)
            pool.wait_ge(pool_const, 14)
            for i in range(1, len(stream)):
                hi, lo = w_parts(i)
                for b in range(2):
                    pool.wait_ge(w_hi_ready, 2 * (i - 1) + b + 1)
                    nc.gpsimd.tensor_tensor(half_cols(lo, b), half_cols(stream[i][1], b), half_cols(hi, b).bitcast(F32),
                                            ALU.subtract).then_inc(w_lo_ready, 1)

        @block.scalar
        def _(act):
            steps = [0]

            def step(ins):
                steps[0] += 1
                ins.then_inc(act_step, 1)
                act.wait_ge(act_step, steps[0])

            for r, src, n in ((0, norm1_g, 8), (8, norm2_g, 8), (32, conv_dw_b, 4), (36, conv_ln_g, 4), (40, conv_ln_b, 4)):
                act.dma_start(rows[r:r + n, :], src.rearrange("(r c) -> r c", c=P)).then_inc(par_in, 16)

            act.wait_ge(pool_const, 1)
            for m in range(MT):
                act.wait_ge(x_in[m], 16)
                step(nc.scalar.activation(junk, hx[:, m, :], ACT.Square, accum_out=st[:, m:m + 1]))
            nc.scalar.activation(st[:, 2:4], st[:, 0:2], ACT.Sqrt, bias=epst[:], scale=1.0 / D).then_inc(ssx, 1)
            act.dma_start(brt[:], b_router.partition_broadcast(P)).then_inc(small_in, 16)
            act.dma_start(wr[:], w_router.rearrange("(k p) n -> p k n", p=P)).then_inc(small_in, 16)
            act.dma_start(bdown[:], b_down).then_inc(small_in, 16)
            for b in range(4):
                freed(act, U_XT + b)
            nc.scalar.activation(u_r[0], uT, ACT.Identity).then_inc(u_hi_ready, 1)

            def weights_high(i, b):
                arrived(act, i)
                nc.scalar.activation(half_cols(w_parts(i)[0], b), half_cols(stream[i][1], b), ACT.Identity).then_inc(w_hi_ready, 1)

            for b in range(2):
                weights_high(1, b)
            for b in range(2):
                u = U_G + b
                full(act, u)
                nc.scalar.activation(aT[:, 2 * b:2 * b + 2, :], bank[u % 4][:].rearrange("p (a b) -> p a b", a=2),
                                     ACT.Identity).then_inc(bank_free[u % 4], 1)
                weights_high(2, b)
            for b in range(2):
                u = U_G + 2 + b
                full(act, u)
                nc.scalar.activation(sq[:, 2 * b:2 * b + 2, :], bank[u % 4][:].rearrange("p (a b) -> p a b", a=2),
                                     ACT.Sigmoid).then_inc(bank_free[u % 4], 1)
                weights_high(3, b)
            for i, t in enumerate((qn, kn)):
                for m in range(MT):
                    u = U_G + 4 + 2 * i + m
                    full(act, u)
                    nc.scalar.activation(t[:, m, :], bank[u % 4][:], ACT.Identity).then_inc(q_copied, 1)
                    for h in range(HEADS):
                        c = i * 16 + m * 8 + h
                        o = m * 512 + h * HD
                        ins = nc.scalar.activation(junk[:, o:o + HD], bank[u % 4][:, h * HD:(h + 1) * HD],
                                                   ACT.Square, accum_out=ssqk[:, c:c + 1])
                    ins.then_inc(bank_free[u % 4], 1)
                    freed(act, u)
                    weights_high(4 + i, m)
            nc.scalar.activation(rqk[:], ssqk[:], ACT.Sqrt, bias=epst[:], scale=1.0 / HD).then_inc(qk_std, 1)
            for m in range(MT):
                u = U_G + 8 + m
                full(act, u)
                nc.scalar.activation(vv[:, m, :], bank[u % 4][:], ACT.Identity).then_inc(bank_free[u % 4], 1)
                weights_high(6, m)

            def gate_bank(b, func):
                u = group_use(5, b)
                full(act, u)
                for c in range(2):
                    k = 2 * b + c
                    ins = nc.scalar.activation(gates[:, k, :], bank[u % 4][:, c * T:(c + 1) * T], func, bias=bgc[:, k:k + 1])
                ins.then_inc(bank_free[u % 4], 1)

            for i in range(16):
                if i % 2 == 1 and i < 13:
                    gate_bank((i - 1) // 2, ACT.Identity)
                if i in (2, 4, 6, 8):
                    b = i // 2 - 1
                    weights_high(7 + b // 2, b % 2)
                if i == 12:
                    for b in range(2):
                        weights_high(ATT_W, b)
                h = i - EXPS
                if 0 <= h < HEADS:
                    act.wait_ge(nmx_ready, h + 1)
                    s = sc[h % 2]
                    nc.scalar.activation(s[:, 0:P], s[:, 0:P], ACT.Exp, bias=nmx[:, h % 2, 0:1], scale=HD ** -0.5,
                                         accum_out=sm[:, h % 2, 0:1]).then_inc(exp_done, 1)
                    nc.scalar.activation(s[:, P:3 * P], s[:, P:3 * P], ACT.Exp, bias=nmx[:, h % 2, 1:2], scale=HD ** -0.5,
                                         accum_out=sm[:, h % 2, 1:2]).then_inc(exp_done, 1)
                if h == HEADS - 1:
                    full(act, U_VAR)
                    nc.scalar.activation(std_c, bank[U_VAR % 4][:, 0:T], ACT.Sqrt, bias=epst[:], scale=1.0 / CC).then_inc(bank_free[U_VAR % 4], 1)
                h = i - EXPS - 1
                if 0 <= h < HEADS:
                    act.wait_ge(t_full, h + 1)
                    if h >= 2:
                        act.wait_ge(pv_done, h - 1)
                    nc.scalar.activation(pT[h % 2], T_BANK[:, 0:384].rearrange("p (a b) -> p a b", a=3),
                                         ACT.Identity).then_inc(t_read, 1)
                c, odd = divmod(i - EXPS - 3, 2)
                if c >= 0 and not odd:
                    act.wait_ge(pv_done, 2 * c + 2)
                    nc.scalar.activation(ao_r[0][:, c, :], O_BANK[:, 0:T], ACT.Identity).then_inc(o_hi, 1)
            act.wait_ge(z_ready, 1)
            nc.scalar.activation(sq, xc, ACT.Sigmoid).then_inc(sig_ready, 1)
            for b in range(6):
                freed(act, group_use(5, b))
            nc.scalar.activation(gates[:, 0:12, :], gates[:, 0:12, :], ACT.Sigmoid).then_inc(gates_ready, 1)
            gate_bank(6, ACT.Sigmoid)
            gate_bank(7, ACT.Sigmoid)
            for b in range(2):
                weights_high(CONV_W, b)
            act.wait_ge(cT_ready, 1)
            nc.scalar.activation(cv_r[0], cv, ACT.Identity).then_inc(cv_hi, 1)
            full(act, U_ATT + 3)
            for b in range(2):
                weights_high(OUT_W, b)
            for b in range(4):
                act.wait_ge(mix_ready, b + 1)
                if b == 0:
                    full(act, LAST_USE[GROUPS - 1])
                nc.scalar.activation(u_r[0][:, 2 * b:2 * b + 2, :], mixT[:, 2 * b:2 * b + 2, :], ACT.Identity).then_inc(mix_hi, 1)
            full(act, U_CONV + 3)
            for b in range(2):
                weights_high(OUT_W + 1, b)

            for j in range(4):
                n, m = divmod(j, 2)
                freed(act, U_OUT + j)
                step(nc.scalar.activation(junk2, hx[:, m, n * 512:(n + 1) * 512], ACT.Square,
                                          accum_out=st[:, 8 + 2 * m + n:9 + 2 * m + n]))
            for m in range(MT):
                step(nc.scalar.activation(st[:, 12 + m:13 + m], st[:, 8 + 2 * m:9 + 2 * m], ACT.Identity, bias=st[:, 9 + 2 * m:10 + 2 * m]))
            nc.scalar.activation(st[:, 14:16], st[:, 12:14], ACT.Sqrt, bias=epst[:], scale=1.0 / D).then_inc(std2, 1)
            for m in range(MT):
                act.wait_ge(v0_ready, m + 1)
                nc.scalar.activation(gt4[:, m, :], top[:, m, 0:TOPK], ACT.Exp, bias=st[:, 16 + m:17 + m],
                                     accum_out=st[:, 18 + m:19 + m]).then_inc(expg, 1)

            act.wait_ge(cum_ready, 1)
            items = act.value_load(cum[0:1, E:E + 1], min_val=1, max_val=ITEMS - 1)
            with act.Fori(0, items) as n:
                act.wait_ge(clip_ready, n + 1)
                nc.scalar.activation(ACT_B, ACT_A, ACT.Sigmoid, scale=ALPHA).then_inc(sigm_ready, 1)
                act.wait_ge(actT_full, n + 1)
                nc.scalar.activation(actT, YB[:].rearrange("p (i s) -> p i s", i=4), ACT.Identity).then_inc(actT_ready, 1)
                act.wait_ge(down_done[3], n + 1)
                act.wait_ge(scattered, n + 1)
                nc.scalar.activation(YR, YB[:], ACT.Identity, scale=gslot[:]).then_inc(y_high, 1)
                act.wait_ge(y_high, 2 * n + 1)
                for half in range(2):
                    r = slice(half * SLOTS, (half + 1) * SLOTS)
                    ins = nc.scalar.activation(ys[0:SLOTS, half, :], YR[r, :], ACT.Identity)
                ins.then_inc(y_high, 1)
            act.wait_ge(scattered, items + 1)
            for m in range(MT):
                nc.scalar.activation(outs[:, m, 0:512], acc[2 * m][:], ACT.Identity).then_inc(out_left, 1)

        @block.vector
        def _(dve):
            steps = [0]

            def done(ins):
                steps[0] += 1
                ins.then_inc(dve_step, 1)
                return steps[0]

            def step(ins):
                dve.wait_ge(dve_step, done(ins))

            full(dve, U_PAR)
            step(nc.vector.tensor_copy(par[:], bank[0][:, 0:46]))
            nc.vector.tensor_copy(dwT[:], bank[0][:, 64:64 + KC * TAPS].rearrange("p (c w) -> p c w", c=KC)).then_inc(bank_free[0], 1)
            dve.wait_ge(ssx, 1)
            step(nc.vector.reciprocal(st[:, 4:6], st[:, 2:4]))
            for m in range(MT):
                nc.vector.tensor_scalar(xn[:, m, :], hx[:, m, :], st[:, 4 + m:5 + m], None, ALU.mult).then_inc(xn_ready, 1)
            for m in range(MT):
                for b in range(2):
                    u = U_XT + 2 * m + b
                    full(dve, u)
                    nc.vector.tensor_tensor(uT[:, 4 * b:4 * b + 4, m * P:(m + 1) * P],
                                            bank[u % 4][:].rearrange("p (a b) -> p a b", a=4),
                                            g1c[:, 4 * b:4 * b + 4].unsqueeze(2).to_broadcast([P, 4, P]),
                                            ALU.mult).then_inc(bank_free[u % 4], 1)

            for b in range(4):
                freed(dve, U_XT + b)
            dve.wait_ge(u_hi_ready, 1)
            nc.vector.tensor_tensor(u_r[1], uT, u_r[0].bitcast(F32), ALU.subtract).then_inc(u_lo_ready, 1)

            dve.wait_ge(pool_const, 6)
            for b in range(2):
                for u in (U_G + b, U_G + 2 + b):
                    freed(dve, u)
                nc.vector.tensor_tensor(hp[:, 2 * b:2 * b + 2, TAPS - 1:], aT[:, 2 * b:2 * b + 2, :],
                                        sq[:, 2 * b:2 * b + 2, :], ALU.mult).then_inc(a_ready, 1)
            dve.wait_ge(a_ready, 2)
            landed = [0] * KC
            for w in range(TAPS):
                for c in range(KC):
                    tap = hp[:, c, w:w + T]
                    if w == 0:
                        landed[c] = done(nc.vector.tensor_scalar(cv[:, c, :], tap, dwT[:, c, 0:1], dwb[:, c:c + 1], ALU.mult, ALU.add))
                    else:
                        dve.wait_ge(dve_step, landed[c])
                        ins = nc.vector.scalar_tensor_tensor(cv[:, c, :], tap, dwT[:, c, w:w + 1], cv[:, c, :], ALU.mult, ALU.add)
                        if w == TAPS - 1 and c == KC - 1:
                            ins.then_inc(cv_done, 1)
                        else:
                            landed[c] = done(ins)
            dve.wait_ge(qk_std, 1)
            nc.vector.reciprocal(rqk[:], rqk[:]).then_inc(rqk_ready, 1)
            dve.wait_ge(rqk_ready, 1)
            dve.wait_ge(q_copied, 4)
            for i, t in enumerate((qn, kn)):
                v = t.rearrange("p m (h d) -> p (m h) d", d=HD)
                f = rqk[:, i * 16:i * 16 + 16].unsqueeze(2).to_broadcast([P, 16, HD])
                nc.vector.tensor_tensor(v, v, f, ALU.mult).then_inc(qk_scaled, 1)

            for j in range(4):
                i, m = divmod(j, 2)
                dve.wait_ge(qkT_full, j + 1)
                nc.vector.tensor_scalar((qT, kT)[i][:, :, m * P:(m + 1) * P], bank[4 + j][:].rearrange("p (a b) -> p a b", a=4),
                                        (qg, kg)[i], None, ALU.mult).then_inc(qkT_ready, 1)
            def attention_low(c):
                dve.wait_ge(o_hi, c + 1)
                nc.vector.tensor_tensor(ao_r[1][:, c, :], O_BANK[:, 0:T], ao_r[0][:, c, :].bitcast(F32), ALU.subtract).then_inc(o_read, 1)

            for h in range(HEADS + 1):
                if h < HEADS:
                    s = sc[h % 2]
                    slope = 2.0 ** (-8.0 * (h + 1) / HEADS)
                    dve.wait_ge(s_full, h + 1)
                    if h >= 2:
                        dve.wait_ge(t_full, h - 1)
                    nc.vector.scalar_tensor_tensor(s, dist, -slope * HD ** 0.5, S_BANKS[h % 2][:, 0:384],
                                                   ALU.mult, ALU.add).then_inc(s_read, 1)
                    dve.wait_ge(s_read, h + 1)
                    done(nc.vector.reduce_max(mx[:, h % 2, 0:1], s[:, 0:P], AX.X))
                    step(nc.vector.reduce_max(mx[:, h % 2, 1:2], s[:, P:3 * P], AX.X))
                    nc.vector.tensor_scalar(nmx[:, h % 2, :], mx[:, h % 2, :], -HD ** -0.5, None, ALU.mult).then_inc(nmx_ready, 1)
                if h >= 1:
                    g = h - 1
                    dve.wait_ge(exp_done, 2 * h)
                    nc.vector.reciprocal(rsm[:, g % 2, :], sm[:, g % 2, :]).then_inc(rsm_ready, 1)
                    dve.wait_ge(rsm_ready, h)
                    s = sc[g % 2]
                    nc.vector.tensor_scalar(s[:, 0:P], s[:, 0:P], rsm[:, g % 2, 0:1], None, ALU.mult).then_inc(p_scaled, 1)
                    nc.vector.tensor_scalar(s[:, P:3 * P], s[:, P:3 * P], rsm[:, g % 2, 1:2], None, ALU.mult).then_inc(p_scaled, 1)
                if h == 1:
                    full(dve, U_MEAN)
                    nc.vector.scalar_tensor_tensor(xc, bank[U_MEAN % 4][:, 0:T].unsqueeze(1).to_broadcast([P, KC, T]), -1.0 / CC, cv,
                                                   ALU.mult, ALU.add).then_inc(bank_free[U_MEAN % 4], 1)
                    freed(dve, U_MEAN)
                    nc.vector.tensor_tensor(sq, xc, xc, ALU.mult).then_inc(sqr_ready, 1)
                if h >= 4 and h % 2 == 0:
                    attention_low((h - 4) // 2)
            freed(dve, U_VAR)
            step(nc.vector.reciprocal(rstd_c, std_c))
            step(nc.vector.tensor_tensor(xc, xc, rstd_c.unsqueeze(1).to_broadcast([P, KC, T]), ALU.mult))
            for c in range(KC):
                ins = nc.vector.tensor_scalar(xc[:, c, :], xc[:, c, :], lng[:, c:c + 1], lnb[:, c:c + 1], ALU.mult, ALU.add)
            ins.then_inc(z_ready, 1)
            dve.wait_ge(z_ready, 1)
            dve.wait_ge(sig_ready, 1)
            nc.vector.tensor_tensor(cv, xc, sq, ALU.mult).then_inc(cT_ready, 1)
            attention_low(3)
            dve.wait_ge(cT_ready, 1)
            dve.wait_ge(cv_hi, 1)
            nc.vector.tensor_tensor(cv_r[1], cv, cv_r[0].bitcast(F32), ALU.subtract).then_inc(cv_lo, 1)

            for b in range(4):
                u = U_ATT + b
                full(dve, u)
                freed(dve, LAST_USE[GROUPS - 1])
                nc.vector.tensor_tensor(mixT[:, 2 * b:2 * b + 2, :], bank[u % 4][:].rearrange("p (a b) -> p a b", a=2),
                                        gates[:, 8 + 2 * b:10 + 2 * b, :], ALU.mult).then_inc(bank_free[u % 4], 1)
            def mix_low(b):
                dve.wait_ge(mix_hi, b + 1)
                m = slice(2 * b, 2 * b + 2)
                nc.vector.tensor_tensor(u_r[1][:, m, :], mixT[:, m, :], u_r[0][:, m, :].bitcast(F32), ALU.subtract).then_inc(mix_lo, 1)

            for b in range(4):
                u = U_CONV + b
                full(dve, u)
                if b >= 1:
                    dve.wait_ge(mix_ready, b)
                nc.vector.tensor_tensor(prod, bank[u % 4][:].rearrange("p (a b) -> p a b", a=2),
                                        gates[:, 2 * b:2 * b + 2, :], ALU.mult).then_inc(bank_free[u % 4], 1)
                freed(dve, u)
                freed(dve, U_ATT + b)
                nc.vector.tensor_tensor(mixT[:, 2 * b:2 * b + 2, :], mixT[:, 2 * b:2 * b + 2, :], prod, ALU.add).then_inc(mix_ready, 1)
                if b >= 1:
                    mix_low(b - 1)
            mix_low(3)
            for j in range(4):
                n, m = divmod(j, 2)
                u = U_OUT + j
                full(dve, u)
                hs = hx[:, m, n * 512:(n + 1) * 512]
                nc.vector.tensor_tensor(hs, hs, bank[u % 4][:], ALU.add).then_inc(bank_free[u % 4], 1)
            dve.wait_ge(std2, 1)
            step(nc.vector.reciprocal(st[:, 6:8], st[:, 14:16]))
            used(dve, OUT_W + 1)
            for m in range(MT):
                nc.vector.tensor_scalar(u2[:, m, :], hx[:, m, :], st[:, 6 + m:7 + m], None, ALU.mult).then_inc(u2_ready, 1)
            for j in range(4):
                m, b = divmod(j, 2)
                u = U_U2T + j
                full(dve, u)
                nc.vector.tensor_tensor(u2T[:, 4 * b:4 * b + 4, m * P:(m + 1) * P],
                                        bank[u % 4][:].rearrange("p (a b) -> p a b", a=4),
                                        g2c[:, 4 * b:4 * b + 4].unsqueeze(2).to_broadcast([P, 4, P]),
                                        ALU.mult).then_inc(bank_free[u % 4], 1)
            full(dve, U_LOG)
            dve.wait_ge(small_in, 48)
            nc.vector.tensor_tensor(lg[:], bank[U_LOG % 4][:, 0:MT * E].rearrange("p (m e) -> p m e", m=MT),
                                    brt[:].unsqueeze(1).to_broadcast([P, MT, E]), ALU.add).then_inc(bank_free[U_LOG % 4], 1)
            freed(dve, U_LOG)
            for m in range(MT):
                step(nc.vector.max(top[:, m, :], lg[:, m, :]))
                nc.vector.tensor_scalar(st[:, 16 + m:17 + m], top[:, m, 0:1], -1.0, None, ALU.mult).then_inc(v0_ready, 1)
                step(nc.vector.max_index(topi[:, m, :], top[:, m, :], lg[:, m, :]))
            step(nc.vector.tensor_copy(topf[:], topi[:]))
            for m in range(MT):
                step(nc.vector.tensor_tensor(eq, iota[:, 0:E].unsqueeze(1).to_broadcast([P, TOPK, E]),
                                             topf[:, m, 0:TOPK].unsqueeze(2).to_broadcast([P, TOPK, E]), ALU.is_equal))
                nc.vector.tensor_reduce(msk[:, m, :], eq.rearrange("p j e -> p e j"), AX.X, ALU.add).then_inc(tab_ready, 1)
                dve.wait_ge(expg, m + 1)
                step(nc.vector.reciprocal(st[:, 18 + m:19 + m], st[:, 18 + m:19 + m]))
                step(nc.vector.tensor_scalar(gt4[:, m, :], gt4[:, m, :], st[:, 18 + m:19 + m], None, ALU.mult))
                dve.wait_ge(tab_ready, m + 1)
                step(nc.vector.tensor_tensor(eq, eq, gt4[:, m, :].unsqueeze(2).to_broadcast([P, TOPK, E]), ALU.mult))
                nc.vector.tensor_reduce(gate[:, m, :], eq.rearrange("p j e -> p e j"), AX.X, ALU.add).then_inc(gTf, 1)
                dve.wait_ge(gTf, m + 1)
            full(dve, U_TAB)
            tb = bank[U_TAB % 4]
            step(nc.vector.scalar_tensor_tensor(pos[:], tb[:, 0:2 * E].rearrange("p (m e) -> p m e", m=MT), 1.0, msk[:], ALU.add, ALU.mult))
            done(nc.vector.tensor_scalar(pos[:], pos[:], -1.0, None, ALU.add))
            cn = tb[0:E, 2 * E:2 * E + 1]
            step(nc.vector.tensor_scalar(tcol[:, 0:1], cn, float(SLOTS), 1.0, ALU.is_gt, ALU.add))
            step(nc.vector.scalar_tensor_tensor(tcol[:, 1:2], cn, 2.0 * SLOTS, tcol[:, 0:1], ALU.is_gt, ALU.add))
            nc.vector.scalar_tensor_tensor(tcol[:, 2:3], cn, 3.0 * SLOTS, tcol[:, 1:2], ALU.is_gt, ALU.add).then_inc(bank_free[U_TAB % 4], 1)
            full(dve, U_ENDS)
            nc.vector.tensor_scalar(past, iota[0:E, 0:ITEMS], bank[U_ENDS % 4][0:E, 0:1], None, ALU.is_ge).then_inc(bank_free[U_ENDS % 4], 1)
            full(dve, U_ITEMS)
            ib = bank[U_ITEMS % 4]
            done(nc.vector.tensor_copy(cum[0:1, T_FIRST:T_FIRST + E + 1], ib[0:1, 0:E + 1]))
            done(nc.vector.tensor_scalar(cum[0:1, T_EXPERT:T_EXPERT + ITEMS], ib[0:1, 64:64 + ITEMS], E - 1.0, None, ALU.min))
            step(nc.vector.tensor_tensor(trow, iota[0:1, 0:ITEMS], ib[0:1, 128:128 + ITEMS], ALU.subtract))
            nc.vector.tensor_scalar(cum[0:1, T_TILE:T_TILE + ITEMS], trow, MAX_TILES - 1.0, None, ALU.min).then_inc(cum_ready, 1)
            full(dve, U_GT)
            dve.wait_ge(seeded, 1)
            nc.vector.tensor_copy(gT, bank[U_GT % 4][0:E, 0:T]).then_inc(gT_ready, 1)
            dve.wait_ge(bup_in, 64)
            b2 = bup.rearrange("p (g f) -> p g f", g=2)
            nc.vector.tensor_copy(bias_r[:], b2).then_inc(bias_hi, 1)
            dve.wait_ge(bias_hi, 1)
            nc.vector.tensor_tensor(bias_r[SLOTS:P], b2[SLOTS:P], bias_r[SLOTS:P].bitcast(F32), ALU.subtract).then_inc(bias_ready, 1)
            nc.vector.memset(ys[:].bitcast(F32), 0.0).then_inc(y_ready, 1)
            nc.vector.memset(hotT[:].bitcast(F32), 0.0).then_inc(hotT_ready, 1)
            nc.vector.memset(ACT_C, 0.0).then_inc(h_free, 1)
            dve.wait_ge(cum_ready, 1)
            dve.wait_ge(pool_const, 14)

            def build(n):
                e = dve.value_load(cum[0:1, bass.ds(n + T_EXPERT, 1)], min_val=0, max_val=E - 1)
                j = dve.value_load(cum[0:1, bass.ds(n + T_TILE, 1)], min_val=0, max_val=MAX_TILES - 1)
                slot = iota[:, bass.ds(j * SLOTS, SLOTS)]
                for m in range(MT):
                    place = pos[:, m, bass.ds(e, 1)]
                    nc.vector.tensor_scalar(hot[:, m, :], slot, place, None, ALU.is_equal).then_inc(hot_ready, 1)
                    nc.vector.tensor_scalar(hotg[:, m, :].rearrange("p (r s) -> p r s", r=2),
                                            slot.unsqueeze(1).to_broadcast([P, 2, SLOTS]),
                                            place, None, ALU.is_equal).then_inc(hot_ready, 1)
                    nc.vector.tensor_scalar(gcur[:, m:m + 1], gate[:, m, bass.ds(e, 1)], 1.0, None, ALU.mult).then_inc(hot_ready, 1)
                nc.vector.tensor_scalar(sel[:], half_of[:], pick[:, bass.ds(e, 1)], None, ALU.mult).then_inc(hot_ready, 1)

            def gathered_to_xt(n):
                dve.wait_ge(gathered, n + 1)
                nc.vector.tensor_tensor(XT, GA[:].rearrange("p (k s) -> p k s", k=KD),
                                        g2c.unsqueeze(2).to_broadcast([P, KD, SLOTS]), ALU.mult).then_inc(xt_ready, 1)

            build(0)
            gathered_to_xt(0)
            items = dve.value_load(cum[0:1, E:E + 1], min_val=1, max_val=ITEMS - 1)
            with dve.Fori(0, items) as n:
                dve.wait_ge(scattered, n + 1)
                nc.vector.tensor_copy(hotT[:], GA[:, 0:T].rearrange("p (m t) -> p m t", m=MT)).then_inc(moe_step, 1)
                nc.vector.tensor_copy(gslot[:], GA[:, T:T + 1]).then_inc(hotT_ready, 1)
                build(n + 1)
                dve.wait_ge(up_done[KD - 1], n + 1)
                nc.vector.tensor_scalar(ACT_A, HG[:], LIMIT, None, ALU.min).then_inc(clip_ready, 1)
                nc.vector.tensor_scalar(ACT_C, HL[:], LIMIT, -LIMIT, ALU.min, ALU.max).then_inc(h_free, 1)
                dve.wait_ge(clip_ready, n + 1)
                dve.wait_ge(h_free, n + 2)
                nc.vector.scalar_tensor_tensor(ACT_C, ACT_C, 1.0, ACT_A, ALU.add, ALU.mult).then_inc(moe_step, 1)
                dve.wait_ge(moe_step, 2 * n + 2)
                dve.wait_ge(sigm_ready, n + 1)
                nc.vector.tensor_tensor(ACT_A, ACT_C, ACT_B, ALU.mult).then_inc(act_ready, 1)
                gathered_to_xt(n + 1)
                dve.wait_ge(y_high, 2 * n + 2)
                dve.wait_ge(y_ready, n + 1)
                for half in range(2):
                    r = slice(half * SLOTS, (half + 1) * SLOTS)
                    ins = nc.vector.tensor_tensor(ys[SLOTS:P, half, :], YR[r, :], ys[0:SLOTS, half, :].bitcast(F32), ALU.subtract)
                ins.then_inc(y_ready, 1)
            dve.wait_ge(scattered, items + 1)
            for m in range(MT):
                nc.vector.tensor_copy(outs[:, m, 512:1024], acc[2 * m + 1][:]).then_inc(out_right, 1)

        @block.tensor
        def _(pe):
            mm = nc.tensor.matmul

            def claim(u):
                if u >= 4:
                    freed(pe, u - 4)

            def product(o, lhs, rhs, n):
                for k in range(n):
                    ins = mm(o, lhs(k), rhs(k), start=(k == 0), stop=(k == n - 1))
                return ins

            pe.wait_ge(pool_const, 1)
            pe.wait_ge(par_in, 16 * 9)
            nc.tensor.transpose(bank[0][:, 0:46], rows, ident[0:46, 0:46])
            for c in range(KC):
                ins = nc.tensor.transpose(bank[0][:, 64 + c * TAPS:64 + (c + 1) * TAPS], dwr[:, c * P:(c + 1) * P], ident[0:TAPS, 0:TAPS])
            ins.then_inc(bank_full[0], 1)
            for m in range(MT):
                pe.wait_ge(xn_ready, m + 1)
                for b in range(2):
                    u = U_XT + 2 * m + b
                    claim(u)
                    for j in range(4):
                        k = 4 * b + j
                        ins = nc.tensor.transpose(bank[u % 4][:, j * P:(j + 1) * P], xn[:, m, k * P:(k + 1) * P], ident[:])
                    ins.then_inc(bank_full[u % 4], 1)

            def product3(o, lhs, rhs, n, before=None):
                for k in range(n):
                    if before:
                        before(k)
                    for i, (a, b) in enumerate(((0, 0), (0, 1), (1, 0))):
                        ins = mm(o, lhs(a, k), rhs(b, k), start=(k == 0 and i == 0), stop=(k == n - 1 and i == 2))
                return ins

            def split(i, b):
                pe.wait_ge(w_lo_ready, 2 * (i - 1) + b + 1)

            def channel_group_bank(i, b, after=None):
                split(i, b)
                w = w_parts(i)
                u = group_use(i, b)
                claim(u)
                for c in range(2):
                    ch = 2 * b + c
                    ins = product3(bank[u % 4][:, c * T:(c + 1) * T], lambda a, k: w[a][:, k, ch * P:(ch + 1) * P],
                                   lambda a, k: u_r[a][:, k, :], KD)
                    if c == 1:
                        ins.then_inc(bank_full[u % 4], 1)
                    elif after:
                        after()

            for b in range(4):
                freed(pe, U_XT + b)
            for b in range(2):
                u = U_G + b
                claim(u)
                for c in range(2):
                    ch = 2 * b + c
                    for k in range(KD):
                        if ch == 0 and k % 2 == 0:
                            pe.wait_ge(g0_in[k // 2], 16)
                        ins = mm(bank[u % 4][:, c * T:(c + 1) * T], stream[0][1][:, k, ch * P:(ch + 1) * P], uT[:, k, :],
                                 start=(k == 0), stop=(k == KD - 1))
                ins.then_inc(bank_full[u % 4], 1)
            pe.wait_ge(u_lo_ready, 1)
            for b in range(2):
                channel_group_bank(1, b)

            def token_group(i, base, before=None):
                w = w_parts(i)
                for b in range(2):
                    split(i, b)
                    for m in range(MT):
                        u = base + m
                        if b == 0:
                            claim(u)
                        ins = product3(bank[u % 4][:, b * T:(b + 1) * T], lambda a, k: u_r[a][:, k, m * P:(m + 1) * P],
                                       lambda a, k: w[a][:, k, b * T:(b + 1) * T], KD, before if b == 0 and m == 0 else None)
                        if b == 1:
                            ins.then_inc(bank_full[u % 4], 1)

            for i in range(2, 5):
                token_group(i, U_G + 2 * i)

            def head(h):
                q0 = (h % 2) * HD
                return slice(q0, q0 + HD), h // 2

            def scores(h):
                r, c = head(h)
                if h < 2:
                    pe.wait_ge(qkT_ready, 4)
                else:
                    pe.wait_ge(s_read, h - 1)
                s = S_BANKS[h % 2]
                mm(s[:, 0:P], qT[r, c, 0:P], kT[r, c, 0:P], start=True, stop=True)
                mm(s[:, P:3 * P], qT[r, c, P:T], kT[r, c, :], start=True, stop=True).then_inc(s_full, 1)

            def transposed_probs(h):
                pe.wait_ge(p_scaled, 2 * h + 2)
                if h >= 1:
                    pe.wait_ge(t_read, h)
                for j in range(3):
                    ins = nc.tensor.transpose(T_BANK[:, j * P:(j + 1) * P], sc[h % 2][:, j * P:(j + 1) * P], ident[:])
                ins.then_inc(t_full, 1)

            def attend(h):
                r, c = head(h)
                pe.wait_ge(t_read, h + 1)
                if h % 2 == 0 and h >= 2:
                    pe.wait_ge(o_read, h // 2)
                p = pT[h % 2]
                v = [vv[:, m, h * HD:(h + 1) * HD] for m in range(MT)]
                mm(O_BANK[r, 0:P], v[0], p[:, 0, :], start=True, stop=True)
                mm(O_BANK[r, P:T], v[0], p[:, 1, :], start=True, stop=False)
                mm(O_BANK[r, P:T], v[1], p[:, 2, :], start=False, stop=True).then_inc(pv_done, 1)

            def qk_transposes():
                pe.wait_ge(qk_scaled, 2)
                for j in range(4):
                    i, m = divmod(j, 2)
                    for c in range(KC):
                        ins = nc.tensor.transpose(bank[4 + j][:, c * P:(c + 1) * P], (qn, kn)[i][:, m, c * P:(c + 1) * P], ident[:])
                    ins.then_inc(qkT_full, 1)

            def between(i):
                if i == SCORES - 1:
                    qk_transposes()
                if 0 <= i - SCORES < HEADS:
                    scores(i - SCORES)
                if 0 <= i - SCORES - 2 < HEADS:
                    transposed_probs(i - SCORES - 2)
                if i == SCORES + 1:
                    pe.wait_ge(cv_done, 1)
                    claim(U_MEAN)
                    product(bank[U_MEAN % 4][:, 0:T], lambda k: ones[:], lambda k: cv[:, k, :], KC).then_inc(bank_full[U_MEAN % 4], 1)
                if i == SCORES + 5:
                    pe.wait_ge(sqr_ready, 1)
                    claim(U_VAR)
                    product(bank[U_VAR % 4][:, 0:T], lambda k: ones[:], lambda k: sq[:, k, :], KC).then_inc(bank_full[U_VAR % 4], 1)
                if 0 <= i - SCORES - 3 < HEADS:
                    if i == SCORES + 3:
                        freed(pe, U_G + 8)
                        freed(pe, U_G + 9)
                    attend(i - SCORES - 3)

            for i in range(5, GROUPS):
                for b in range(2):
                    slot = 4 * (i - 5) + 2 * b
                    channel_group_bank(i, b, lambda: between(slot))
                    between(slot + 1)

            def branch(i, base, src, b):
                if b % 2 == 0:
                    split(i, b // 2)
                w = w_parts(i)
                u = base + b
                claim(u)
                for c in range(2):
                    ch = 2 * b + c
                    ins = product3(bank[u % 4][:, c * T:(c + 1) * T], lambda a, k: w[a][:, k, ch * P:(ch + 1) * P],
                                   lambda a, k: src[a][:, k, :], KC)
                ins.then_inc(bank_full[u % 4], 1)

            pe.wait_ge(o_read, KC)
            for b in range(4):
                branch(ATT_W, U_ATT, ao_r, b)
            pe.wait_ge(cv_lo, 1)
            for b in range(4):
                branch(CONV_W, U_CONV, cv_r, b)
            for n in range(2):
                token_group(OUT_W + n, U_OUT + 2 * n,
                            (lambda k: pe.wait_ge(mix_lo, k // 2 + 1)) if n == 0 else None)
            for j in range(4):
                freed(pe, U_OUT + j)
            for m in range(MT):
                for n in range(2):
                    ins = mm(acc[2 * m + n][:], ident[:], hx[:, m, n * 512:(n + 1) * 512], start=True, stop=False, skip_group_check=True)
            ins.then_inc(seeded, 1)
            for m in range(MT):
                pe.wait_ge(u2_ready, m + 1)
                for b in range(2):
                    u = U_U2T + 2 * m + b
                    claim(u)
                    for j in range(4):
                        k = 4 * b + j
                        ins = nc.tensor.transpose(bank[u % 4][:, j * P:(j + 1) * P], u2[:, m, k * P:(k + 1) * P], ident[:])
                    ins.then_inc(bank_full[u % 4], 1)
            for b in range(4):
                freed(pe, U_U2T + b)
            pe.wait_ge(small_in, 48)
            claim(U_LOG)
            for m in range(MT):
                ins = product(bank[U_LOG % 4][:, m * E:(m + 1) * E], lambda k: u2T[:, k, m * P:(m + 1) * P], lambda k: wr[:, k, :], KD)
            ins.then_inc(bank_full[U_LOG % 4], 1)
            pe.wait_ge(tab_ready, MT)
            claim(U_TAB)
            tb = bank[U_TAB % 4]
            mm(tb[:, 0:E], tri[:], msk[:, 0, :], start=True, stop=True)
            mm(tb[:, E:2 * E], ones[:], msk[:, 0, :], start=True, stop=False)
            mm(tb[:, E:2 * E], tri[:], msk[:, 1, :], start=False, stop=True)
            mm(tb[0:E, 2 * E:2 * E + 1], msk[:, 0, :], ones[:, 0:1], start=True, stop=False)
            mm(tb[0:E, 2 * E:2 * E + 1], msk[:, 1, :], ones[:, 0:1], start=False, stop=True).then_inc(bank_full[U_TAB % 4], 1)
            pe.wait_ge(gTf, MT)
            claim(U_GT)
            for m in range(MT):
                ins = mm(bank[U_GT % 4][0:E, m * P:(m + 1) * P], gate[:, m, :], ident[:], start=True, stop=True)
            ins.then_inc(bank_full[U_GT % 4], 1)
            freed(pe, U_TAB)
            claim(U_ENDS)
            mm(bank[U_ENDS % 4][0:E, 0:1], tri[0:E, 0:E], tcol[:, 2:3], start=True, stop=False)
            mm(bank[U_ENDS % 4][0:E, 0:1], ident[0:E, 0:E], tcol[:, 2:3], start=False, stop=True).then_inc(bank_full[U_ENDS % 4], 1)
            freed(pe, U_ENDS)
            claim(U_ITEMS)
            ib = bank[U_ITEMS % 4]
            mm(ib[0:1, 0:E + 1], tcol[:, 2:3], tri[0:E, 0:E + 1], start=True, stop=True)
            mm(ib[0:1, 64:64 + ITEMS], ones[0:E, 0:1], past, start=True, stop=True)
            mm(ib[0:1, 128:128 + ITEMS], tcol[:, 2:3], past, start=True, stop=True).then_inc(bank_full[U_ITEMS % 4], 1)
            pe.wait_ge(gT_ready, 1)
            for m in range(MT):
                for n in range(2):
                    mm(acc[2 * m + n][:], gT[:, m * P:(m + 1) * P], bdown[:, n * 512:(n + 1) * 512],
                       start=False, stop=False, skip_group_check=True)

            def scatter():
                for m in range(MT):
                    for half in range(2):
                        ins = mm(acc[2 * m + half][:], hotT[:, m, :], ys[:, half, :], start=False, stop=False, skip_group_check=True)
                ins.then_inc(scattered, 1)

            def gather(n):
                pe.wait_ge(hot_ready, 7 * n + 7)
                for k in range(KD):
                    for m in range(MT):
                        ins = mm(GA[:, k * SLOTS:(k + 1) * SLOTS], u2[:, m, k * P:(k + 1) * P], hot[:, m, :],
                                 start=(m == 0), stop=(m == MT - 1))
                ins.then_inc(gathered, 1)

            pe.wait_ge(bias_ready, 1)
            pe.wait_ge(cum_ready, 1)
            freed(pe, U_LOG)
            gather(0)
            places = [(b_[half * SLOTS:(half + 1) * SLOTS, :], (2 * g + half) * 512)
                      for g, b_ in enumerate((HG, HL)) for half in range(2)]
            with pe.Fori(0, E // 2) as pair:
                for a in range(2):
                    e = pe.snap(2 * pair + a)
                    first = pe.value_load(cum[0:1, bass.ds(e, 1)], min_val=0, max_val=ITEMS - 1)
                    end = pe.value_load(cum[0:1, bass.ds(e + 1, 1)], min_val=1, max_val=ITEMS - 1)
                    with pe.Fori(first, end) as n:
                        pe.wait_ge(xt_ready, n + 1)
                        for m in range(MT):
                            nc.tensor.transpose(GA[:, m * P:(m + 1) * P], hotg[:, m, :], ident[:])
                        mm(GA[:, T:T + 1], hotg[:, 0, :], gcur[:, 0:1], start=True, stop=False)
                        mm(GA[:, T:T + 1], hotg[:, 1, :], gcur[:, 1:2], start=False, stop=True)
                        pe.wait_ge(h_free, n + 1)
                        for g, b_ in enumerate((HG, HL)):
                            mm(b_[:], sel[:], bias_r[:, g, :], start=True, stop=False, skip_group_check=True)
                        for k in range(KD):
                            pe.wait_ge(up_in[a][k], 16 * pair + 16)
                            for o, f in places:
                                ins = mm(o, XT[:, k, :], up[a][:, k, f:f + 512], start=False, stop=(k == KD - 1), skip_group_check=True)
                            ins.then_inc(up_done[k], 1)
                            if k == 1:
                                pe.wait_ge(y_ready, n + 1)
                                pe.wait_ge(hotT_ready, n + 1)
                                scatter()
                        gather(n + 1)
                        pe.wait_ge(act_ready, n + 1)
                        for i in range(4):
                            ins = nc.tensor.transpose(YB[:, i * P:(i + 1) * P], ACT_A[:, i * P:(i + 1) * P], ident[:])
                        ins.then_inc(actT_full, 1)
                        pe.wait_ge(actT_ready, n + 1)
                        for c in range(4):
                            pe.wait_ge(down_in[c], 16 * e + 16)
                            for k in (2 * c, 2 * c + 1):
                                for half in range(2):
                                    ins = mm(YB[half * SLOTS:(half + 1) * SLOTS, :], actT[:, k % 4, (k // 4) * SLOTS:(k // 4 + 1) * SLOTS],
                                             down[:, k, half * 512:(half + 1) * 512], start=(k == 0), stop=(k == KD - 1), skip_group_check=True)
                            ins.then_inc(down_done[c], 1)
            items = pe.value_load(cum[0:1, E:E + 1], min_val=1, max_val=ITEMS - 1)
            pe.wait_ge(y_ready, items + 1)
            pe.wait_ge(hotT_ready, items + 1)
            scatter()


_INS = ["x", "norm1_g", "w_in", "b_gates", "conv_dw", "conv_dw_b", "conv_ln_g", "conv_ln_b", "w_conv_out",
        "q_norm_g", "k_norm_g", "w_attn_out", "w_out", "norm2_g", "w_router", "b_router",
        "w_up_gate", "b_up_gate", "w_down", "b_down"]


def kernel(**inputs):
    import numpy as np
    import concourse.bacc as bacc
    from concourse.bass_utils import run_bass_kernel_spmd

    nc = bacc.Bacc("TRN2", target_bir_lowering=False, num_devices=1, dynamic_dma_scratch_size=1024)
    arrays, args = {}, []
    for name in _INS:
        a = np.ascontiguousarray(inputs[name])
        a = a.reshape(a.shape[1:])
        arrays["in_" + name] = a
        args.append(nc.dram_tensor("in_" + name, a.shape, mybir.dt.from_np(a.dtype), kind="ExternalInput").ap())
    result = nc.dram_tensor("out_0", (T, D), F32, kind="ExternalOutput").ap()
    hybrid_block(nc, *args, result)
    r = run_bass_kernel_spmd(nc, [arrays], core_ids=[0])
    return r.results[0]["out_0"].reshape(1, T, D)
```

```python
import concourse.bass as bass
from concourse import mybir
from contextlib import ExitStack

F32 = mybir.dt.float32
F32R = mybir.dt.float32r
I32 = mybir.dt.int32
U32 = mybir.dt.uint32
ALU = mybir.AluOpType
ACT = mybir.ActivationFunctionType
AX = mybir.AxisListType

P = 128
T = 256
MT = T // P
D = 1024
KD = D // P
CC = 512
KC = CC // P
TAPS = 31
HEADS = 8
HD = 64
E = 32
TOPK = 4
FF = 1024
LIMIT = 7.0
ALPHA = 1.702
EPS = 1e-6
SLOTS = 64
MAX_TILES = T // SLOTS
ITEMS = TOPK * T // SLOTS + E + 1
T_FIRST, T_EXPERT, T_TILE, T_ORDER = 0, E + 1, E + 1 + ITEMS, E + 1 + 2 * ITEMS
TABLE = T_ORDER + E
WIDE_FIRST, WIDE_EVERY = 7, 4
SWITCH = 3
DOWN_ORDER = (0, 2, 1, 3)
GROUPS = 9
FAR = 1e30


def hybrid_block(nc, x, norm1_g, w_in, b_gates, conv_dw, conv_dw_b, conv_ln_g, conv_ln_b, w_conv_out,
                 q_norm_g, k_norm_g, w_attn_out, w_out, norm2_g, w_router, b_router,
                 w_up_gate, b_up_gate, w_down, b_down, out):
    ctx = ExitStack()
    with ctx:
        def sb(name, shape, dt=F32):
            return ctx.enter_context(nc.sbuf_tensor(name, shape, dt))

        def sem(name):
            return ctx.enter_context(nc.semaphore(name))

        def sb_placed(name, columns):
            t = sb(name, [P, columns])
            return t, nc.sbuf_base - 4 * columns

        UP_EVEN, EVEN_AT = sb_placed("up_even", KD * 2 * FF)
        UP_ODD, ODD_AT = sb_placed("up_odd", KD * 2 * FF)
        DOWN, DOWN_AT = sb_placed("down", KD * D)
        up = [r[:, :].rearrange("p (k n) -> p k n", k=KD) for r in (UP_EVEN, UP_ODD)]
        down = DOWN[:, :].rearrange("p (k n) -> p k n", k=KD)
        REG_H = sb("reg_h", [P, 2048])
        REG_U = sb("reg_u", [P, 2048])
        REG_E, E_AT = sb_placed("reg_e", 4096)
        REG_R = sb("reg_r", [P, 1152])

        slots = [REG_E[:, :], DOWN[:, 0:4096], DOWN[:, 4096:8192]]

        def part(name, at, column, n):
            return nc.alloc_sbuf_tensor_at(name, [P, n], F32R, offset=at + 4 * column)

        w_lo = [part("w_lo0", E_AT, 0, 4096), part("w_lo1", DOWN_AT, 0, 4096), part("w_lo2", DOWN_AT, 4096, 4096)]
        w_hi = [part("w_hi0", EVEN_AT, 0, 4096), part("w_hi1", EVEN_AT, 4096, 4096)]
        u_r = [part(n, EVEN_AT, 8192 + 2048 * i, 2048)[:, :].rearrange("p (k t) -> p k t", k=KD)
               for i, n in enumerate(("u_hi", "u_lo"))]
        ao_r = [part(n, ODD_AT, 10240 + 1024 * i, 1024)[:, :].rearrange("p (k t) -> p k t", k=KC)
                for i, n in enumerate(("ao_hi", "ao_lo"))]
        cv_r = [part(n, ODD_AT, 4096 + 1024 * i, 1024)[:, :].rearrange("p (k t) -> p k t", k=KC)
                for i, n in enumerate(("cv_hi", "cv_lo"))]

        def tmp(at, n, **kw):
            v = UP_ODD[:, at:at + n]
            return v.rearrange("p (a b) -> p a b", **kw) if kw else v

        gates = tmp(0, 4096, a=16)
        junk = tmp(2048, 1024)
        aT = tmp(4096, 1024, a=KC)
        hp = tmp(5120, KC * (T + TAPS - 1), a=KC)
        cv = tmp(6272, 1024, a=KC)
        xc = tmp(7296, 1024, a=KC)
        sq = tmp(8320, 1024, a=KC)
        std_c = tmp(9344, 256)
        rstd_c = tmp(9600, 256)
        dist = tmp(9856, 384)
        qn = tmp(10240, 1024, a=MT)
        kn = tmp(11264, 1024, a=MT)
        vv = tmp(12288, 1024, a=MT)
        qT = tmp(13312, 1024, a=KC)
        kT = tmp(14336, 1024, a=KC)
        pT = [tmp(15360 + 384 * i, 384, a=3) for i in range(2)]
        prod = REG_R[:, 0:512].rearrange("p (a b) -> p a b", a=2)

        hx = REG_H[:, :].rearrange("p (m d) -> p m d", m=MT)
        uT = REG_U[:, :].rearrange("p (k t) -> p k t", k=KD)
        mixT = uT
        u2T = uT
        u2 = REG_E[:, 0:2048].rearrange("p (m d) -> p m d", m=MT)
        bup = REG_E[:, 2048:3072]
        rows = REG_R[0:46, 512:640]
        dwr = REG_R[0:TAPS, 0:512]
        sc = [REG_R[:, 384 * i:384 * i + 384] for i in range(3)]
        junk2 = REG_R[:, 0:1024]
        eq = REG_R[:, 512:768].rearrange("p (m j e) -> p m j e", m=MT, j=TOPK)
        eqg = REG_R[:, 768:1024].rearrange("p (m j e) -> p m j e", m=MT, j=TOPK)
        trow = REG_R[0:1, 1088:1088 + ITEMS]
        past = REG_R[0:E, 1024:1024 + ITEMS]

        ACT_A, ACT_B, ACT_C, YR = [REG_H[:, 512 * i:512 * i + 512] for i in range(4)]
        actT = REG_U[:, 0:512].rearrange("p (i s) -> p i s", i=4)
        XT = REG_R[:, 0:512].rearrange("p (k s) -> p k s", k=KD)
        hot = REG_R[:, 512:640].rearrange("p (m s) -> p m s", m=MT)
        hotg = REG_R[:, 640:896].rearrange("p (m s) -> p m s", m=MT)
        outs = UP_EVEN[:, 0:2048].rearrange("p (m d) -> p m d", m=MT)

        bdown = sb("bdown", [E, D])
        gT = sb("gates_t", [E, T])
        wr = sb("wr", [P, KD, E])
        ident = sb("ident", [P, P])
        tri = sb("tri", [P, P])
        ones = sb("ones", [P, P])
        iota = sb("iota", [P, T])
        par = sb("par", [P, 46])
        dwT = sb("dwT", [P, KC, TAPS])
        epst = sb("epst", [P, 1])
        st = sb("st", [P, 24])
        ssqk = sb("ssqk", [P, 2 * MT * HEADS])
        rqk = sb("rqk", [P, 2 * MT * HEADS])
        mx = sb("mx", [P, 2, 2])
        nmx = sb("nmx", [P, 2, 2])
        sm = sb("sm", [P, 2, 2])
        rsm = sb("rsm", [P, 2, 2])
        brt = sb("brt", [P, E])
        lg = sb("lg", [P, MT, E])
        top = sb("top", [P, MT, 8])
        topi = sb("topi", [P, MT, 8], U32)
        topf = sb("topf", [P, MT, 8])
        gt4 = sb("gt4", [P, MT, TOPK])
        gate = sb("gate", [P, MT, E])
        msk = sb("msk", [P, MT, E])
        pos = sb("pos", [P, MT, E])
        tcol = sb("tcol", [E, 3])
        wide = sb("wide", [E, 1])
        key = sb("key", [E, 4])
        turn = sb("turn", [E, 1])
        before = sb("before", [E, E])
        at_turn = sb("at_turn", [E, E + 1])
        exp_col = sb("exp_col", [E, 3])
        by_turn = sb("by_turn", [E, 2])
        later = sb("later", [E, 1])
        cum = sb("cum", [1, TABLE], I32)
        pick = sb("pick", [P, E])
        half_of = sb("half_of", [P, P])
        gcur = sb("gcur", [P, MT])
        gslot = sb("gslot", [P, 1])
        bias_r = sb("bias_r", [P, 2, 512], F32R)
        sel = sb("sel", [P, P], F32R)
        ys = sb("ys", [P, 2, 512], F32R)
        hotT = sb("hotT", [P, MT, P], F32R)

        g1c, g2c = par[:, 0:8], par[:, 8:16]
        bgc, dwb, lng, lnb = par[:, 16:32], par[:, 32:36], par[:, 36:40], par[:, 40:44]
        qg, kg = par[:, 44:45], par[:, 45:46]

        bank = [ctx.enter_context(nc.psum_tensor(f"bank{i}", [P, 512], F32)) for i in range(8)]
        HG, HL, GA, YB = bank[0:4]
        ACT_T = [HG[:, 0:256], HL[:, 0:256]]

        def half_row(t, c):
            return t[:, 256 * c:256 * c + 256]

        S_BANKS, T_BANK, O_BANK = bank[4:6], bank[6], bank[7]
        PAR_BANK, RSTD_BANK = bank[4:6]
        acc = bank[4:8]

        def sems(names):
            return [sem(n) for n in names.split()]

        par_in, small_in, bup_in, out_sem = sems("par_in small_in bup_in out_sem")
        x_in = [sem(f"x_in{m}") for m in range(MT)]
        slot_in = [sem(f"slot_in{i}") for i in range(3)]
        g0_in = [sem(f"g0_in{c}") for c in range(4)]
        up_in = [[sem(f"up_in{a}_{c}") for c in range(KD)] for a in range(2)]
        down_in = [sem(f"down_in{c}") for c in range(4)]
        pool_const, expert_const = sems("pool_const expert_const")
        act_step, dve_step, pool_step = sems("act_step dve_step pool_step")
        bank_full = [sem(f"bank_full{i}") for i in range(4)]
        bank_free = [sem(f"bank_free{i}") for i in range(4)]
        ssx, rstd_ready, rstd_row, par_full, par_ready = sems("ssx rstd_ready rstd_row par_full par_ready")
        w_hi_ready, w_lo_ready, u_hi_ready, u_lo_ready = sems("w_hi_ready w_lo_ready u_hi_ready u_lo_ready")
        mix_hi, mix_lo, cv_hi, cv_lo, o_hi = sems("mix_hi mix_lo cv_hi cv_lo o_hi")
        q_copied, qk_std, rqk_ready, qk_scaled, qkT_full, qkT_ready = sems("q_copied qk_std rqk_ready qk_scaled qkT_full qkT_ready")
        s_full, s_read, nmx_ready, exp_done, rsm_ready = sems("s_full s_read nmx_ready exp_done rsm_ready")
        p_scaled, t_full, t_read, pv_done, o_read = sems("p_scaled t_full t_read pv_done o_read")
        a_ready, cv_done, sqr_ready, z_ready, sig_ready, cT_ready = sems("a_ready cv_done sqr_ready z_ready sig_ready cT_ready")
        gates_ready, mix_ready = sems("gates_ready mix_ready")
        std2, rstd2, u2_ready, v0_ready, expg, tab_ready = sems("std2 rstd2 u2_ready v0_ready expg tab_ready")
        gate_ready, wide_ready, cum_ready, seeded, bias_hi, bias_ready = sems("gate_ready wide_ready cum_ready seeded bias_hi bias_ready")
        hot_ready, gathered, xt_ready, scattered, hotT_ready = sems("hot_ready gathered xt_ready scattered hotT_ready")
        up_done = [sem(f"up_done{c}") for c in range(KD)]
        down_done = [sem(f"down_done{c}") for c in range(4)]
        clip_ready, lin_ready, sigm_ready, act_ready, actT_full, actT_ready = sems(
            "clip_ready lin_ready sigm_ready act_ready actT_full actT_ready")
        y_high, y_ready, moe_step = sems("y_high y_ready moe_step")
        out_left, out_right = sems("out_left out_right")

        block = ctx.enter_context(nc.Block())

        win = w_in.rearrange("(k p) n -> p k n", p=P)
        stream = [(win[:, :, 512 * i:512 * i + 512], slots[i % 3].rearrange("p (k n) -> p k n", k=KD))
                  for i in range(GROUPS)]
        ATT_W, CONV_W, OUT_W = GROUPS, GROUPS + 1, GROUPS + 2
        stream.append((w_attn_out.rearrange("(k p) n -> p k n", p=P),
                       slots[ATT_W % 3].rearrange("p (k n) -> p k n", k=KC)))
        stream.append((w_conv_out.rearrange("(k p) n -> p k n", p=P),
                       slots[CONV_W % 3].rearrange("p (k n) -> p k n", k=KC)))
        wout = w_out.rearrange("(k p) n -> p k n", p=P)
        for half in range(2):
            stream.append((wout[:, :, 512 * half:512 * half + 512],
                           slots[(OUT_W + half) % 3].rearrange("p (k n) -> p k n", k=KD)))

        def w_parts(i):
            k = stream[i][1].shape[1]
            return [t[:, :].rearrange("p (k n) -> p k n", k=k) for t in (w_hi[i % 2], w_lo[i % 3])]

        def half_cols(w, b):
            n = w.shape[2] // 2
            return w[:, :, b * n:(b + 1) * n]

        def arrived(eng, i):
            eng.wait_ge(slot_in[i % 3], 16 * (i // 3 + (1 if i % 3 else 0)))

        U_XT = 0
        U_G = U_XT + 4

        def group_use(i, b):
            b += 2 * i
            return U_G + b + (b > 15) + (b > 16)

        U_MEAN, U_VAR = U_G + 16, U_G + 18
        U_ATT = U_G + 2 * GROUPS + 2
        U_CONV = U_ATT + 4
        U_OUT = U_CONV + 4
        U_U2T = U_OUT + 4
        U_LOG = U_U2T + 4
        U_TAB = U_LOG + 1
        U_WIDE = U_TAB + 2
        U_GT = U_TAB + 3
        U_KEYS = U_TAB + 4
        U_TURN = U_TAB + 6
        U_ENDS = U_TAB + 7
        U_ITEMS = U_TAB + 8

        SCORES = 2
        EXPS = SCORES + 1
        LAST_USE = [group_use(i, 1) for i in range(GROUPS)] + [U_ATT + 3, U_CONV + 3, U_OUT + 1, U_OUT + 3]

        def full(eng, u):
            eng.wait_ge(bank_full[u % 4], u // 4 + 1)

        def freed(eng, u):
            eng.wait_ge(bank_free[u % 4], u // 4 + 1)

        def used(eng, i):
            full(eng, LAST_USE[i])

        @block.sync
        def _(sp):
            for m in range(MT):
                sp.dma_start(hx[:, m, :], x[m * P:(m + 1) * P, :]).then_inc(x_in[m], 16)
            sp.dma_start(dwr, conv_dw).then_inc(par_in, 16)
            sp.dma_start(rows[16:32, :], b_gates.rearrange("(r c) -> r c", c=P)).then_inc(par_in, 16)
            for r, src in ((44, q_norm_g), (45, k_norm_g)):
                sp.dma_start(rows[r:r + 1, :].rearrange("r (h d) -> r h d", h=2),
                             src.rearrange("(r h d) -> r h d", r=1, h=1).to_broadcast([1, 2, HD])).then_inc(par_in, 16)

            def load_up(par_, c, e):
                sp.dma_start(up[par_][:, c, :], w_up_gate[e, c * P:(c + 1) * P, :]).then_inc(up_in[par_][c], 16)

            def load_down(c, e):
                sp.dma_start(down[:, 2 * c:2 * c + 2, :],
                             w_down[e, 2 * c * P:(2 * c + 2) * P, :].rearrange("(r p) n -> p r n", p=P)
                             ).then_inc(down_in[c], 16)

            for i, (src, dst) in enumerate(stream):
                if i >= 3:
                    used(sp, i - 3)
                if i == 0:
                    for c in range(4):
                        sp.dma_start(dst[:, 2 * c:2 * c + 2, :], src[:, 2 * c:2 * c + 2, :]).then_inc(g0_in[c], 16)
                else:
                    sp.dma_start(dst, src).then_inc(slot_in[i % 3], 16)
                if i in (4, 5):
                    load_up(0, i + 2, 0)
                if i == CONV_W:
                    sp.wait_ge(pv_done, HEADS)
                    load_up(1, 6, 1)
                    load_up(1, 7, 1)
            load_up(1, 5, 1)
            sp.wait_ge(cv_lo, 1)
            load_up(1, 3, 1)
            load_up(1, 4, 1)
            used(sp, CONV_W)
            load_down(0, 0)
            load_down(1, 0)
            sp.wait_ge(mix_ready, 4)
            for c in range(3):
                load_up(1, c, 1)
            used(sp, OUT_W)
            load_up(0, 2, 0)
            load_up(0, 3, 0)
            used(sp, OUT_W + 1)
            for q in range(4):
                sp.dma_start(bup[q * E:(q + 1) * E, :].rearrange("e (g f) -> e g f", g=2),
                             b_up_gate.rearrange("e (g h f) -> e g h f", g=2, h=2)[:, :, q % 2, :]).then_inc(bup_in, 16)
            for c in (0, 1, 4, 5):
                load_up(0, c, 0)
            load_down(2, 0)
            load_down(3, 0)
            sp.wait_ge(cum_ready, 1)
            def expert_of(t):
                return sp.value_load(cum[0:1, bass.ds(t + T_ORDER, 1)], min_val=0, max_val=E - 1)

            def items_before(t):
                return sp.value_load(cum[0:1, bass.ds(t + T_FIRST, 1)], min_val=1, max_val=ITEMS - 1)

            def fetch_up(a, e, items):
                for c in range(KD):
                    sp.wait_ge(up_done[c], items)
                    sp.dma_start(up[a][:, c, :], w_up_gate[bass.ds(e, 1), c * P:(c + 1) * P, :].rearrange("e p n -> p (e n)")
                                 ).then_inc(up_in[a][c], 16)

            def fetch_down(e, items):
                for c in DOWN_ORDER:
                    sp.wait_ge(down_done[c], items)
                    sp.dma_start(down[:, 2 * c:2 * c + 2, :],
                                 w_down[bass.ds(e, 1), 2 * c * P:(2 * c + 2) * P, :].rearrange("e (r p) n -> p (e r) n", p=P)
                                 ).then_inc(down_in[c], 16)

            with sp.Fori(1, SWITCH) as pair:
                for a in range(2):
                    t = sp.snap(2 * pair + a)
                    items = items_before(t - 1)
                    fetch_up(a, expert_of(t), items)
                    fetch_down(expert_of(t - 1), items)
            with sp.Fori(SWITCH, E // 2) as pair:
                for a in range(2):
                    t = sp.snap(2 * pair + a)
                    items = items_before(t - 1)
                    fetch_down(expert_of(t - 1), items)
                    fetch_up(a, expert_of(t), items)
            fetch_down(expert_of(E - 1), items_before(E - 1))
            for m in range(MT):
                sp.wait_ge(out_left, m + 1)
                sp.wait_ge(out_right, m + 1)
                sp.dma_start(out[m * P:(m + 1) * P, :], outs[:, m, :]).then_inc(out_sem, 16)
            sp.wait_ge(out_sem, 16 * MT)

        @block.gpsimd
        def _(pool):
            nc.gpsimd.memset(ones[:], 1.0).then_inc(pool_step, 1)
            nc.gpsimd.memset(epst[:], EPS).then_inc(pool_step, 1)
            pool.wait_ge(pool_step, 2)
            nc.gpsimd.affine_select(out=ident[:], in_=ones[:], compare_op=ALU.is_equal, fill=0.0,
                                    base=0, pattern=[[-1, P]], channel_multiplier=1).then_inc(pool_const, 1)
            nc.gpsimd.affine_select(out=tri[:], in_=ones[:], compare_op=ALU.is_gt, fill=0.0,
                                    base=0, pattern=[[1, P]], channel_multiplier=-1).then_inc(pool_const, 1)
            nc.gpsimd.iota(iota[:], [[1, T]], base=0, channel_multiplier=0,
                           allow_small_or_imprecise_dtypes=True).then_inc(pool_const, 1)
            nc.gpsimd.iota(dist[:, 0:P], [[-1, P]], base=0, channel_multiplier=1,
                           allow_small_or_imprecise_dtypes=True).then_inc(pool_step, 1)
            nc.gpsimd.iota(dist[:, P:3 * P], [[-1, T]], base=P, channel_multiplier=1,
                           allow_small_or_imprecise_dtypes=True).then_inc(pool_step, 1)
            pool.wait_ge(pool_step, 4)
            nc.gpsimd.affine_select(out=dist[:, 0:P], in_=dist[:, 0:P], compare_op=ALU.is_ge, fill=FAR,
                                    base=0, pattern=[[-1, P]], channel_multiplier=1).then_inc(pool_const, 1)
            nc.gpsimd.affine_select(out=dist[:, P:3 * P], in_=dist[:, P:3 * P], compare_op=ALU.is_ge, fill=FAR,
                                    base=P, pattern=[[-1, T]], channel_multiplier=1).then_inc(pool_const, 1)
            nc.gpsimd.memset(hp, 0.0).then_inc(pool_const, 1)
            nc.gpsimd.iota(exp_col[:, 1:2], [[0, 1]], base=0, channel_multiplier=1,
                           allow_small_or_imprecise_dtypes=True).then_inc(expert_const, 1)
            nc.gpsimd.iota(exp_col[:, 2:3], [[0, 1]], base=0, channel_multiplier=-1,
                           allow_small_or_imprecise_dtypes=True).then_inc(expert_const, 1)
            pool.wait_ge(expert_const, 2)
            nc.gpsimd.tensor_scalar(later[:], exp_col[:, 1:2], 2.0, None, ALU.is_ge).then_inc(expert_const, 1)
            nc.gpsimd.memset(half_of[:], 0.0).then_inc(pool_step, 1)
            pool.wait_ge(pool_step, 5)
            for q in range(4):
                pool.wait_ge(pool_const, 6 + 2 * q)
                nc.gpsimd.tensor_copy(pick[q * E:(q + 1) * E, :], ident[0:E, 0:E]).then_inc(pool_const, 1)
                c = (q % 2) * SLOTS
                pool.wait_ge(pool_const, 7 + 2 * q)
                nc.gpsimd.memset(half_of[q * E:(q + 1) * E, c:c + SLOTS], 1.0).then_inc(pool_const, 1)
            pool.wait_ge(pool_const, 14)
            for i in range(1, len(stream)):
                hi, lo = w_parts(i)
                for b in range(2):
                    pool.wait_ge(w_hi_ready, 2 * (i - 1) + b + 1)
                    nc.gpsimd.tensor_tensor(half_cols(lo, b), half_cols(stream[i][1], b), half_cols(hi, b).bitcast(F32),
                                            ALU.subtract).then_inc(w_lo_ready, 1)
            pool.wait_ge(bup_in, 64)
            b2 = bup.rearrange("p (g f) -> p g f", g=2)
            nc.gpsimd.tensor_copy(bias_r[:], b2).then_inc(bias_hi, 1)
            pool.wait_ge(bias_hi, 1)
            nc.gpsimd.tensor_tensor(bias_r[SLOTS:P], b2[SLOTS:P], bias_r[SLOTS:P].bitcast(F32), ALU.subtract).then_inc(bias_ready, 1)

        @block.scalar
        def _(act):
            steps = [0]

            def step(ins):
                steps[0] += 1
                ins.then_inc(act_step, 1)
                act.wait_ge(act_step, steps[0])

            for r, src, n in ((0, norm1_g, 8), (8, norm2_g, 8), (32, conv_dw_b, 4), (36, conv_ln_g, 4), (40, conv_ln_b, 4)):
                act.dma_start(rows[r:r + n, :], src.rearrange("(r c) -> r c", c=P)).then_inc(par_in, 16)

            act.wait_ge(pool_const, 1)
            step(nc.scalar.activation(st[:, 2:3], epst[:], ACT.Sqrt))
            for m in range(MT):
                act.wait_ge(x_in[m], 16)
                step(nc.scalar.activation(junk, hx[:, m, :], ACT.Square, accum_out=st[:, m:m + 1]))
            nc.scalar.activation(st[:, 2:4], st[:, 0:2], ACT.Sqrt, bias=epst[:], scale=1.0 / D).then_inc(ssx, 1)
            act.dma_start(brt[:], b_router.partition_broadcast(P)).then_inc(small_in, 16)
            act.dma_start(wr[:], w_router.rearrange("(k p) n -> p k n", p=P)).then_inc(small_in, 16)
            act.dma_start(bdown[:], b_down).then_inc(small_in, 16)
            for b in range(4):
                freed(act, U_XT + b)
            nc.scalar.activation(u_r[0], uT, ACT.Identity).then_inc(u_hi_ready, 1)

            def weights_high(i, b):
                arrived(act, i)
                nc.scalar.activation(half_cols(w_parts(i)[0], b), half_cols(stream[i][1], b), ACT.Identity).then_inc(w_hi_ready, 1)

            for b in range(2):
                weights_high(1, b)
            for b in range(2):
                u = U_G + b
                full(act, u)
                nc.scalar.activation(aT[:, 2 * b:2 * b + 2, :], bank[u % 4][:].rearrange("p (a b) -> p a b", a=2),
                                     ACT.Identity).then_inc(bank_free[u % 4], 1)
                weights_high(2, b)
            for b in range(2):
                u = U_G + 2 + b
                full(act, u)
                nc.scalar.activation(sq[:, 2 * b:2 * b + 2, :], bank[u % 4][:].rearrange("p (a b) -> p a b", a=2),
                                     ACT.Sigmoid).then_inc(bank_free[u % 4], 1)
                weights_high(3, b)
            for i, t in enumerate((qn, kn)):
                for m in range(MT):
                    u = U_G + 4 + 2 * i + m
                    full(act, u)
                    nc.scalar.activation(t[:, m, :], bank[u % 4][:], ACT.Identity).then_inc(q_copied, 1)
                    for h in range(HEADS):
                        c = i * 16 + m * 8 + h
                        o = m * 512 + h * HD
                        ins = nc.scalar.activation(junk[:, o:o + HD], bank[u % 4][:, h * HD:(h + 1) * HD],
                                                   ACT.Square, accum_out=ssqk[:, c:c + 1])
                    ins.then_inc(bank_free[u % 4], 1)
                    freed(act, u)
                    weights_high(4 + i, m)
            nc.scalar.activation(rqk[:], ssqk[:], ACT.Sqrt, bias=epst[:], scale=1.0 / HD).then_inc(qk_std, 1)
            for m in range(MT):
                u = U_G + 8 + m
                full(act, u)
                nc.scalar.activation(vv[:, m, :], bank[u % 4][:], ACT.Identity).then_inc(bank_free[u % 4], 1)
                weights_high(6, m)

            def gate_bank(b, func):
                u = group_use(5, b)
                full(act, u)
                for c in range(2):
                    k = 2 * b + c
                    ins = nc.scalar.activation(gates[:, k, :], bank[u % 4][:, c * T:(c + 1) * T], func, bias=bgc[:, k:k + 1])
                ins.then_inc(bank_free[u % 4], 1)

            for i in range(16):
                if i % 2 == 1 and i < 13:
                    gate_bank((i - 1) // 2, ACT.Identity)
                if i in (2, 4, 6, 8):
                    b = i // 2 - 1
                    weights_high(7 + b // 2, b % 2)
                if i == 12:
                    for b in range(2):
                        weights_high(ATT_W, b)
                h = i - EXPS
                if 0 <= h < HEADS:
                    act.wait_ge(nmx_ready, h + 1)
                    s = sc[h % 3]
                    nc.scalar.activation(s[:, 0:P], s[:, 0:P], ACT.Exp, bias=nmx[:, h % 2, 0:1], scale=HD ** -0.5,
                                         accum_out=sm[:, h % 2, 0:1]).then_inc(exp_done, 1)
                    nc.scalar.activation(s[:, P:3 * P], s[:, P:3 * P], ACT.Exp, bias=nmx[:, h % 2, 1:2], scale=HD ** -0.5,
                                         accum_out=sm[:, h % 2, 1:2]).then_inc(exp_done, 1)
                h = i - EXPS - 1
                if 0 <= h < HEADS:
                    act.wait_ge(rsm_ready, h + 1)
                    s = sc[h % 3]
                    nc.scalar.activation(s[:, 0:P], s[:, 0:P], ACT.Identity, scale=rsm[:, h % 2, 0:1]).then_inc(p_scaled, 1)
                    nc.scalar.activation(s[:, P:3 * P], s[:, P:3 * P], ACT.Identity, scale=rsm[:, h % 2, 1:2]).then_inc(p_scaled, 1)
                h = i - EXPS - 2
                if 0 <= h < HEADS:
                    act.wait_ge(t_full, h + 1)
                    if h >= 2:
                        act.wait_ge(pv_done, h - 1)
                    nc.scalar.activation(pT[h % 2], T_BANK[:, 0:384].rearrange("p (a b) -> p a b", a=3),
                                         ACT.Identity).then_inc(t_read, 1)
                c, odd = divmod(i - EXPS - 4, 2)
                if 0 <= c < KC and not odd:
                    act.wait_ge(pv_done, 2 * c + 2)
                    nc.scalar.activation(ao_r[0][:, c, :], O_BANK[:, 0:T], ACT.Identity).then_inc(o_hi, 1)
            for b in range(6):
                freed(act, group_use(5, b))
            nc.scalar.activation(gates[:, 0:12, :], gates[:, 0:12, :], ACT.Sigmoid).then_inc(gates_ready, 1)
            full(act, U_VAR)
            nc.scalar.activation(std_c, bank[U_VAR % 4][:, 0:T], ACT.Sqrt, bias=epst[:], scale=1.0 / CC).then_inc(bank_free[U_VAR % 4], 1)
            gate_bank(6, ACT.Sigmoid)
            gate_bank(7, ACT.Sigmoid)
            weights_high(CONV_W, 0)
            act.wait_ge(z_ready, 1)
            nc.scalar.activation(sq, xc, ACT.Sigmoid).then_inc(sig_ready, 1)
            weights_high(CONV_W, 1)
            act.wait_ge(cT_ready, 1)
            nc.scalar.activation(cv_r[0], cv, ACT.Identity).then_inc(cv_hi, 1)
            full(act, U_ATT + 3)
            for b in range(2):
                weights_high(OUT_W, b)
            for b in range(4):
                act.wait_ge(mix_ready, b + 1)
                if b == 0:
                    full(act, LAST_USE[GROUPS - 1])
                nc.scalar.activation(u_r[0][:, 2 * b:2 * b + 2, :], mixT[:, 2 * b:2 * b + 2, :], ACT.Identity).then_inc(mix_hi, 1)
            full(act, U_CONV + 3)
            for b in range(2):
                weights_high(OUT_W + 1, b)

            for m in range(MT):
                freed(act, U_OUT + 2 + m)
                step(nc.scalar.activation(junk2, hx[:, m, :], ACT.Square, accum_out=st[:, 12 + m:13 + m]))
            nc.scalar.activation(st[:, 14:16], st[:, 12:14], ACT.Sqrt, bias=epst[:], scale=1.0 / D).then_inc(std2, 1)
            act.wait_ge(rstd2, 1)
            used(act, OUT_W + 1)
            for m in range(MT):
                nc.scalar.activation(u2[:, m, :], hx[:, m, :], ACT.Identity, scale=st[:, 6 + m:7 + m]).then_inc(u2_ready, 1)
            act.wait_ge(v0_ready, 1)
            for m in range(MT):
                ins = nc.scalar.activation(gt4[:, m, :], top[:, m, 0:TOPK], ACT.Exp, bias=st[:, 16 + m:17 + m],
                                           accum_out=st[:, 18 + m:19 + m])
            ins.then_inc(expg, 1)

            act.wait_ge(cum_ready, 1)
            items = act.value_load(cum[0:1, E:E + 1], min_val=1, max_val=ITEMS - 1)
            with act.Fori(0, items) as n:
                for c in range(2):
                    act.wait_ge(clip_ready, 2 * n + c + 1)
                    nc.scalar.activation(half_row(ACT_B, c), half_row(ACT_A, c), ACT.Sigmoid, scale=ALPHA).then_inc(sigm_ready, 1)
                for c in range(2):
                    act.wait_ge(actT_full, 2 * n + c + 1)
                    nc.scalar.activation(actT[:, 2 * c:2 * c + 2, :], ACT_T[c].rearrange("p (i s) -> p i s", i=2),
                                         ACT.Identity).then_inc(actT_ready, 1)
                act.wait_ge(down_done[3], n + 1)
                act.wait_ge(scattered, n + 1)
                nc.scalar.activation(YR, YB[:], ACT.Identity, scale=gslot[:]).then_inc(y_high, 1)
                act.wait_ge(y_high, 2 * n + 1)
                for half in range(2):
                    r = slice(half * SLOTS, (half + 1) * SLOTS)
                    ins = nc.scalar.activation(ys[0:SLOTS, half, :], YR[r, :], ACT.Identity)
                ins.then_inc(y_high, 1)
            act.wait_ge(scattered, items + 1)
            for m in range(MT):
                nc.scalar.activation(outs[:, m, 0:512], acc[2 * m][:], ACT.Identity).then_inc(out_left, 1)

        @block.vector
        def _(dve):
            steps = [0]

            def done(ins):
                steps[0] += 1
                ins.then_inc(dve_step, 1)
                return steps[0]

            def step(ins):
                dve.wait_ge(dve_step, done(ins))

            nc.vector.memset(ys[:].bitcast(F32), 0.0).then_inc(y_ready, 1)
            nc.vector.memset(hotT[:].bitcast(F32), 0.0).then_inc(hotT_ready, 1)
            dve.wait_ge(par_full, 1)
            nc.vector.tensor_copy(par[:], PAR_BANK[:, 0:46]).then_inc(par_ready, 1)
            nc.vector.tensor_copy(dwT[:], PAR_BANK[:, 64:64 + KC * TAPS].rearrange("p (c w) -> p c w", c=KC)).then_inc(par_ready, 1)
            dve.wait_ge(ssx, 1)
            nc.vector.reciprocal(st[:, 4:6], st[:, 2:4]).then_inc(rstd_ready, 1)
            dve.wait_ge(par_ready, 2)
            dve.wait_ge(rstd_row, 1)
            step(nc.vector.tensor_copy(rstd_c, RSTD_BANK[:, 0:T]))
            for b in range(4):
                u = U_XT + b
                full(dve, u)
                for k in (2 * b, 2 * b + 1):
                    ins = nc.vector.scalar_tensor_tensor(uT[:, k, :], bank[u % 4][:, k % 2 * T:(k % 2 + 1) * T], g1c[:, k:k + 1],
                                                         rstd_c, ALU.mult, ALU.mult)
                ins.then_inc(bank_free[u % 4], 1)
            for b in range(4):
                freed(dve, U_XT + b)
            dve.wait_ge(u_hi_ready, 1)
            nc.vector.tensor_tensor(u_r[1], uT, u_r[0].bitcast(F32), ALU.subtract).then_inc(u_lo_ready, 1)

            dve.wait_ge(pool_const, 6)
            for b in range(2):
                for u in (U_G + b, U_G + 2 + b):
                    freed(dve, u)
                nc.vector.tensor_tensor(hp[:, 2 * b:2 * b + 2, TAPS - 1:], aT[:, 2 * b:2 * b + 2, :],
                                        sq[:, 2 * b:2 * b + 2, :], ALU.mult).then_inc(a_ready, 1)
            dve.wait_ge(a_ready, 2)
            landed = [0] * KC
            def taps(first, end):
                for w in range(first, end):
                    for c in range(KC):
                        tap = hp[:, c, w:w + T]
                        if w == 0:
                            landed[c] = done(nc.vector.tensor_scalar(cv[:, c, :], tap, dwT[:, c, 0:1], dwb[:, c:c + 1], ALU.mult, ALU.add))
                        else:
                            dve.wait_ge(dve_step, landed[c])
                            ins = nc.vector.scalar_tensor_tensor(cv[:, c, :], tap, dwT[:, c, w:w + 1], cv[:, c, :], ALU.mult, ALU.add)
                            if w == TAPS - 1 and c == KC - 1:
                                ins.then_inc(cv_done, 1)
                            else:
                                landed[c] = done(ins)

            early_taps = 20
            taps(0, early_taps)
            dve.wait_ge(qk_std, 1)
            nc.vector.reciprocal(rqk[:], rqk[:]).then_inc(rqk_ready, 1)
            dve.wait_ge(rqk_ready, 1)
            dve.wait_ge(q_copied, 4)
            for i, t in enumerate((qn, kn)):
                v = t.rearrange("p m (h d) -> p (m h) d", d=HD)
                f = rqk[:, i * 16:i * 16 + 16].unsqueeze(2).to_broadcast([P, 16, HD])
                nc.vector.tensor_tensor(v, v, f, ALU.mult).then_inc(qk_scaled, 1)

            for j in range(4):
                i, m = divmod(j, 2)
                dve.wait_ge(qkT_full, j + 1)
                nc.vector.tensor_scalar((qT, kT)[i][:, :, m * P:(m + 1) * P], bank[4 + j][:].rearrange("p (a b) -> p a b", a=4),
                                        (qg, kg)[i], None, ALU.mult).then_inc(qkT_ready, 1)
            def attention_low(c):
                dve.wait_ge(o_hi, c + 1)
                nc.vector.tensor_tensor(ao_r[1][:, c, :], O_BANK[:, 0:T], ao_r[0][:, c, :].bitcast(F32), ALU.subtract).then_inc(o_read, 1)

            for h in range(HEADS + 1):
                if h < HEADS:
                    s = sc[h % 3]
                    slope = 2.0 ** (-8.0 * (h + 1) / HEADS)
                    dve.wait_ge(s_full, h + 1)
                    if h >= 3:
                        dve.wait_ge(t_full, h - 2)
                    nc.vector.scalar_tensor_tensor(s, dist, -slope * HD ** 0.5, S_BANKS[h % 2][:, 0:384],
                                                   ALU.mult, ALU.add).then_inc(s_read, 1)
                    dve.wait_ge(s_read, h + 1)
                    done(nc.vector.reduce_max(mx[:, h % 2, 0:1], s[:, 0:P], AX.X))
                    step(nc.vector.reduce_max(mx[:, h % 2, 1:2], s[:, P:3 * P], AX.X))
                    nc.vector.tensor_scalar(nmx[:, h % 2, :], mx[:, h % 2, :], -HD ** -0.5, None, ALU.mult).then_inc(nmx_ready, 1)
                if h >= 1:
                    g = h - 1
                    dve.wait_ge(exp_done, 2 * h)
                    if g >= 2:
                        dve.wait_ge(p_scaled, 2 * g - 2)
                    nc.vector.reciprocal(rsm[:, g % 2, :], sm[:, g % 2, :]).then_inc(rsm_ready, 1)
                if h < HEADS:
                    taps(*[early_taps + (TAPS - early_taps) * (h + i) // HEADS for i in range(2)])
                if h >= 4 and h % 2 == 0:
                    attention_low((h - 4) // 2)
            full(dve, U_MEAN)
            dve.wait_ge(cv_done, 1)
            nc.vector.scalar_tensor_tensor(xc, bank[U_MEAN % 4][:, 0:T].unsqueeze(1).to_broadcast([P, KC, T]), -1.0 / CC, cv,
                                           ALU.mult, ALU.add).then_inc(bank_free[U_MEAN % 4], 1)
            freed(dve, U_MEAN)
            nc.vector.tensor_tensor(sq, xc, xc, ALU.mult).then_inc(sqr_ready, 1)
            attention_low(3)
            freed(dve, U_VAR)
            step(nc.vector.reciprocal(rstd_c, std_c))
            step(nc.vector.tensor_tensor(xc, xc, rstd_c.unsqueeze(1).to_broadcast([P, KC, T]), ALU.mult))
            for c in range(KC):
                ins = nc.vector.tensor_scalar(xc[:, c, :], xc[:, c, :], lng[:, c:c + 1], lnb[:, c:c + 1], ALU.mult, ALU.add)
            ins.then_inc(z_ready, 1)
            dve.wait_ge(z_ready, 1)
            dve.wait_ge(sig_ready, 1)
            nc.vector.tensor_tensor(cv, xc, sq, ALU.mult).then_inc(cT_ready, 1)
            dve.wait_ge(cT_ready, 1)
            dve.wait_ge(cv_hi, 1)
            nc.vector.tensor_tensor(cv_r[1], cv, cv_r[0].bitcast(F32), ALU.subtract).then_inc(cv_lo, 1)

            for b in range(4):
                u = U_ATT + b
                full(dve, u)
                freed(dve, LAST_USE[GROUPS - 1])
                nc.vector.tensor_tensor(mixT[:, 2 * b:2 * b + 2, :], bank[u % 4][:].rearrange("p (a b) -> p a b", a=2),
                                        gates[:, 8 + 2 * b:10 + 2 * b, :], ALU.mult).then_inc(bank_free[u % 4], 1)
            def mix_low(b):
                dve.wait_ge(mix_hi, b + 1)
                m = slice(2 * b, 2 * b + 2)
                nc.vector.tensor_tensor(u_r[1][:, m, :], mixT[:, m, :], u_r[0][:, m, :].bitcast(F32), ALU.subtract).then_inc(mix_lo, 1)

            for b in range(4):
                u = U_CONV + b
                full(dve, u)
                if b >= 1:
                    dve.wait_ge(mix_ready, b)
                nc.vector.tensor_tensor(prod, bank[u % 4][:].rearrange("p (a b) -> p a b", a=2),
                                        gates[:, 2 * b:2 * b + 2, :], ALU.mult).then_inc(bank_free[u % 4], 1)
                freed(dve, u)
                freed(dve, U_ATT + b)
                nc.vector.tensor_tensor(mixT[:, 2 * b:2 * b + 2, :], mixT[:, 2 * b:2 * b + 2, :], prod, ALU.add).then_inc(mix_ready, 1)
                if b >= 1:
                    mix_low(b - 1)
            mix_low(3)
            def add_to_h(n, m):
                u = U_OUT + 2 * n + m
                full(dve, u)
                hs = hx[:, m, n * 512:(n + 1) * 512]
                nc.vector.tensor_tensor(hs, hs, bank[u % 4][:], ALU.add).then_inc(bank_free[u % 4], 1)

            for m in range(MT):
                add_to_h(0, m)
            for m in range(MT):
                add_to_h(1, m)
                for b in range(2):
                    u = U_U2T + 2 * m + b
                    full(dve, u)
                    nc.vector.tensor_tensor(u2T[:, 4 * b:4 * b + 4, m * P:(m + 1) * P],
                                            bank[u % 4][:].rearrange("p (a b) -> p a b", a=4),
                                            g2c[:, 4 * b:4 * b + 4].unsqueeze(2).to_broadcast([P, 4, P]),
                                            ALU.mult).then_inc(bank_free[u % 4], 1)
            dve.wait_ge(std2, 1)
            nc.vector.reciprocal(st[:, 6:8], st[:, 14:16]).then_inc(rstd2, 1)
            dve.wait_ge(rstd2, 1)
            def build_hot(slot, e):
                for m in range(MT):
                    nc.vector.tensor_scalar(hot[:, m, :], slot, pos[:, m, e], None, ALU.is_equal).then_inc(hot_ready, 1)

            def build_rest(slot, e):
                for m in range(MT):
                    nc.vector.tensor_scalar(hotg[:, m, :].rearrange("p (r s) -> p r s", r=2),
                                            slot.unsqueeze(1).to_broadcast([P, 2, SLOTS]),
                                            pos[:, m, e], None, ALU.is_equal).then_inc(hot_ready, 1)
                    nc.vector.tensor_scalar(gcur[:, m:m + 1], gate[:, m, e], 1.0, None, ALU.mult).then_inc(hot_ready, 1)
                nc.vector.tensor_scalar(sel[:], half_of[:], pick[:, e], None, ALU.mult).then_inc(hot_ready, 1)

            full(dve, U_LOG)
            dve.wait_ge(small_in, 48)
            for m in range(MT):
                ins = nc.vector.scalar_tensor_tensor(lg[:, m, :], bank[U_LOG % 4][:, m * E:(m + 1) * E], st[:, 6 + m:7 + m],
                                                     brt[:], ALU.mult, ALU.add)
            ins.then_inc(bank_free[U_LOG % 4], 1)
            freed(dve, U_LOG)
            for m in range(MT):
                last = done(nc.vector.max(top[:, m, :], lg[:, m, :]))
            dve.wait_ge(dve_step, last)
            nc.vector.tensor_scalar(st[:, 16:18], top[:, :, 0], -1.0, None, ALU.mult).then_inc(v0_ready, 1)
            for m in range(MT):
                last = done(nc.vector.max_index(topi[:, m, :], top[:, m, :], lg[:, m, :]))
            dve.wait_ge(dve_step, last)
            step(nc.vector.tensor_copy(topf[:], topi[:]))
            full_shape = [P, MT, TOPK, E]
            step(nc.vector.tensor_tensor(eq, iota[:, 0:E].unsqueeze(1).unsqueeze(1).to_broadcast(full_shape),
                                         topf[:, :, 0:TOPK].unsqueeze(3).to_broadcast(full_shape), ALU.is_equal))
            nc.vector.tensor_reduce(msk[:], eq.rearrange("p m j e -> p m e j"), AX.X, ALU.add).then_inc(tab_ready, 1)
            dve.wait_ge(expg, 1)
            step(nc.vector.reciprocal(st[:, 18:20], st[:, 18:20]))
            step(nc.vector.tensor_tensor(gt4[:], gt4[:], st[:, 18:20].unsqueeze(2).to_broadcast([P, MT, TOPK]), ALU.mult))
            step(nc.vector.tensor_tensor(eqg, eq, gt4[:].unsqueeze(3).to_broadcast(full_shape), ALU.mult))
            nc.vector.tensor_reduce(gate[:], eqg.rearrange("p m j e -> p m e j"), AX.X, ALU.add).then_inc(gate_ready, 1)
            full(dve, U_TAB)
            tb = bank[U_TAB % 4]
            cn = tb[0:E, 2 * E:2 * E + 1]
            step(nc.vector.tensor_scalar(tcol[:, 0:1], cn, float(SLOTS), 1.0, ALU.is_gt, ALU.add))
            dve.wait_ge(expert_const, 3)
            nc.vector.tensor_scalar(wide[:], cn, float(SLOTS), later[:], ALU.is_gt, ALU.mult).then_inc(wide_ready, 1)
            step(nc.vector.scalar_tensor_tensor(tcol[:, 1:2], cn, 2.0 * SLOTS, tcol[:, 0:1], ALU.is_gt, ALU.add))
            step(nc.vector.scalar_tensor_tensor(exp_col[:, 0:1], cn, 3.0 * SLOTS, tcol[:, 1:2], ALU.is_gt, ALU.add))
            dve.wait_ge(tab_ready, 1)
            nc.vector.scalar_tensor_tensor(pos[:], tb[:, 0:2 * E].rearrange("p (m e) -> p m e", m=MT), 1.0, msk[:],
                                           ALU.add, ALU.mult).then_inc(bank_free[U_TAB % 4], 1)
            freed(dve, U_TAB)
            step(nc.vector.tensor_scalar(pos[:], pos[:], -1.0, None, ALU.add))
            full(dve, U_WIDE)
            w = bank[U_WIDE % 4][0:E, 0:1]
            step(nc.vector.scalar_tensor_tensor(key[:, 0:1], exp_col[:, 1:2], -2.0, w, ALU.add, ALU.subtract))
            step(nc.vector.tensor_scalar(key[:, 1:2], w, float(WIDE_EVERY), WIDE_FIRST + 0.5, ALU.mult, ALU.add))
            step(nc.vector.tensor_scalar(key[:, 2:3], key[:, 1:2], key[:, 0:1], wide[:], ALU.subtract, ALU.mult))
            nc.vector.tensor_tensor(key[:, 3:4], key[:, 2:3], key[:, 0:1], ALU.add).then_inc(bank_free[U_WIDE % 4], 1)
            full(dve, U_GT)
            nc.vector.tensor_copy(gT[:], bank[U_GT % 4][0:E, 0:T]).then_inc(bank_free[U_GT % 4], 1)
            build_hot(iota[:, 0:SLOTS], slice(0, 1))
            freed(dve, U_WIDE)
            full(dve, U_KEYS)
            step(nc.vector.tensor_scalar(before[:], bank[U_KEYS % 4][0:E, 0:E], key[:, 3:4], None, ALU.is_lt))
            step(nc.vector.tensor_reduce(turn[:], before[:], AX.X, ALU.add))
            nc.vector.tensor_scalar(at_turn[:], iota[0:E, 0:E + 1], turn[:], None, ALU.is_equal).then_inc(bank_free[U_KEYS % 4], 1)
            full(dve, U_TURN)
            nc.vector.tensor_copy(by_turn[:], bank[U_TURN % 4][0:E, 0:2]).then_inc(bank_free[U_TURN % 4], 1)
            full(dve, U_ENDS)
            nc.vector.tensor_scalar(past, iota[0:E, 0:ITEMS], bank[U_ENDS % 4][0:E, 0:1], None, ALU.is_ge).then_inc(bank_free[U_ENDS % 4], 1)
            dve.wait_ge(pool_const, 14)
            build_rest(iota[:, 0:SLOTS], slice(0, 1))
            full(dve, U_ITEMS)
            ib = bank[U_ITEMS % 4]
            done(nc.vector.tensor_copy(cum[0:1, T_FIRST:T_FIRST + E + 1], ib[0:1, 0:E + 1]))
            done(nc.vector.tensor_copy(cum[0:1, T_EXPERT:T_EXPERT + ITEMS], ib[0:1, 64:64 + ITEMS]))
            done(nc.vector.tensor_copy(cum[0:1, T_ORDER:T_ORDER + E], ib[0:1, 192:192 + E]))
            step(nc.vector.tensor_tensor(trow, iota[0:1, 0:ITEMS], ib[0:1, 128:128 + ITEMS], ALU.subtract))
            nc.vector.tensor_scalar(cum[0:1, T_TILE:T_TILE + ITEMS], trow, MAX_TILES - 1.0, None, ALU.min).then_inc(cum_ready, 1)
            def build(n):
                e = dve.value_load(cum[0:1, bass.ds(n + T_EXPERT, 1)], min_val=0, max_val=E - 1)
                j = dve.value_load(cum[0:1, bass.ds(n + T_TILE, 1)], min_val=0, max_val=MAX_TILES - 1)
                slot = iota[:, bass.ds(j * SLOTS, SLOTS)]
                build_hot(slot, bass.ds(e, 1))
                build_rest(slot, bass.ds(e, 1))

            def gathered_to_xt(n):
                dve.wait_ge(gathered, n + 1)
                nc.vector.tensor_tensor(XT, GA[:].rearrange("p (k s) -> p k s", k=KD),
                                        g2c.unsqueeze(2).to_broadcast([P, KD, SLOTS]), ALU.mult).then_inc(xt_ready, 1)

            dve.wait_ge(cum_ready, 1)
            dve.wait_ge(seeded, 1)
            gathered_to_xt(0)
            items = dve.value_load(cum[0:1, E:E + 1], min_val=1, max_val=ITEMS - 1)
            with dve.Fori(0, items) as n:
                dve.wait_ge(scattered, n + 1)
                nc.vector.tensor_copy(hotT[:], GA[:, 0:T].rearrange("p (m t) -> p m t", m=MT)).then_inc(moe_step, 1)
                nc.vector.tensor_copy(gslot[:], GA[:, T:T + 1]).then_inc(hotT_ready, 1)
                build(n + 1)
                dve.wait_ge(up_done[KD - 1], n + 1)
                def clip_gate(c):
                    nc.vector.tensor_scalar(half_row(ACT_A, c), half_row(HG, c), LIMIT, None, ALU.min).then_inc(clip_ready, 1)

                def clip_linear(c):
                    nc.vector.tensor_scalar(half_row(ACT_C, c), half_row(HL, c), LIMIT, -LIMIT, ALU.min, ALU.max).then_inc(lin_ready, 1)

                def multiply(c):
                    dve.wait_ge(lin_ready, 2 * n + c + 1)
                    dve.wait_ge(clip_ready, 2 * n + c + 1)
                    nc.vector.scalar_tensor_tensor(half_row(ACT_C, c), half_row(ACT_C, c), 1.0, half_row(ACT_A, c),
                                                   ALU.add, ALU.mult).then_inc(moe_step, 1)
                    dve.wait_ge(moe_step, 3 * n + c + 2)
                    dve.wait_ge(sigm_ready, 2 * n + c + 1)
                    nc.vector.tensor_tensor(half_row(ACT_A, c), half_row(ACT_C, c), half_row(ACT_B, c), ALU.mult).then_inc(act_ready, 1)

                clip_gate(0)
                clip_linear(0)
                clip_gate(1)
                multiply(0)
                clip_linear(1)
                multiply(1)
                gathered_to_xt(n + 1)
                dve.wait_ge(y_high, 2 * n + 2)
                dve.wait_ge(y_ready, n + 1)
                for half in range(2):
                    r = slice(half * SLOTS, (half + 1) * SLOTS)
                    ins = nc.vector.tensor_tensor(ys[SLOTS:P, half, :], YR[r, :], ys[0:SLOTS, half, :].bitcast(F32), ALU.subtract)
                ins.then_inc(y_ready, 1)
            dve.wait_ge(scattered, items + 1)
            for m in range(MT):
                nc.vector.tensor_copy(outs[:, m, 512:1024], acc[2 * m + 1][:]).then_inc(out_right, 1)

        @block.tensor
        def _(pe):
            mm = nc.tensor.matmul

            def claim(u):
                if u >= 4:
                    freed(pe, u - 4)

            def product(o, lhs, rhs, n):
                for k in range(n):
                    ins = mm(o, lhs(k), rhs(k), start=(k == 0), stop=(k == n - 1))
                return ins

            pe.wait_ge(pool_const, 1)
            for m in range(MT):
                pe.wait_ge(x_in[m], 16)
                for b in range(4):
                    for k in (2 * b, 2 * b + 1):
                        c = k % 2 * T + m * P
                        ins = nc.tensor.transpose(bank[(U_XT + b) % 4][:, c:c + P], hx[:, m, k * P:(k + 1) * P], ident[:])
                    if m == MT - 1:
                        ins.then_inc(bank_full[(U_XT + b) % 4], 1)
            pe.wait_ge(par_in, 16 * 9)
            nc.tensor.transpose(PAR_BANK[:, 0:46], rows, ident[0:46, 0:46])
            for c in range(KC):
                ins = nc.tensor.transpose(PAR_BANK[:, 64 + c * TAPS:64 + (c + 1) * TAPS], dwr[:, c * P:(c + 1) * P], ident[0:TAPS, 0:TAPS])
            ins.then_inc(par_full, 1)
            pe.wait_ge(rstd_ready, 1)
            for m in range(MT):
                ins = mm(RSTD_BANK[:, m * P:(m + 1) * P], st[:, 4 + m:5 + m].to_broadcast([P, P]), ident[:], start=True, stop=True)
            ins.then_inc(rstd_row, 1)

            def product3(o, lhs, rhs, n, before=None):
                for k in range(n):
                    if before:
                        before(k)
                    for i, (a, b) in enumerate(((0, 0), (0, 1), (1, 0))):
                        ins = mm(o, lhs(a, k), rhs(b, k), start=(k == 0 and i == 0), stop=(k == n - 1 and i == 2))
                return ins

            def split(i, b):
                pe.wait_ge(w_lo_ready, 2 * (i - 1) + b + 1)

            def channel_group_bank(i, b, after=None):
                split(i, b)
                w = w_parts(i)
                u = group_use(i, b)
                claim(u)
                for c in range(2):
                    ch = 2 * b + c
                    ins = product3(bank[u % 4][:, c * T:(c + 1) * T], lambda a, k: w[a][:, k, ch * P:(ch + 1) * P],
                                   lambda a, k: u_r[a][:, k, :], KD)
                    if c == 1:
                        ins.then_inc(bank_full[u % 4], 1)
                    elif after:
                        after()

            for b in range(2):
                u = U_G + b
                claim(u)
                for c in range(2):
                    ch = 2 * b + c
                    for k in range(KD):
                        if ch == 0 and k % 2 == 0:
                            freed(pe, U_XT + k // 2)
                            pe.wait_ge(g0_in[k // 2], 16)
                        ins = mm(bank[u % 4][:, c * T:(c + 1) * T], stream[0][1][:, k, ch * P:(ch + 1) * P], uT[:, k, :],
                                 start=(k == 0), stop=(k == KD - 1))
                ins.then_inc(bank_full[u % 4], 1)
            pe.wait_ge(u_lo_ready, 1)
            for b in range(2):
                channel_group_bank(1, b)

            def token_group(i, base, before=None):
                w = w_parts(i)
                for b in range(2):
                    split(i, b)
                    for m in range(MT):
                        u = base + m
                        if b == 0:
                            claim(u)
                        ins = product3(bank[u % 4][:, b * T:(b + 1) * T], lambda a, k: u_r[a][:, k, m * P:(m + 1) * P],
                                       lambda a, k: w[a][:, k, b * T:(b + 1) * T], KD, before if b == 0 and m == 0 else None)
                        if b == 1:
                            ins.then_inc(bank_full[u % 4], 1)

            for i in range(2, 5):
                token_group(i, U_G + 2 * i)

            def head(h):
                q0 = (h % 2) * HD
                return slice(q0, q0 + HD), h // 2

            def scores(h):
                r, c = head(h)
                if h < 2:
                    pe.wait_ge(qkT_ready, 4)
                else:
                    pe.wait_ge(s_read, h - 1)
                s = S_BANKS[h % 2]
                mm(s[:, 0:P], qT[r, c, 0:P], kT[r, c, 0:P], start=True, stop=True)
                mm(s[:, P:3 * P], qT[r, c, P:T], kT[r, c, :], start=True, stop=True).then_inc(s_full, 1)

            def transposed_probs(h):
                pe.wait_ge(p_scaled, 2 * h + 2)
                if h >= 1:
                    pe.wait_ge(t_read, h)
                for j in range(3):
                    ins = nc.tensor.transpose(T_BANK[:, j * P:(j + 1) * P], sc[h % 3][:, j * P:(j + 1) * P], ident[:])
                ins.then_inc(t_full, 1)

            def attend(h):
                r, c = head(h)
                pe.wait_ge(t_read, h + 1)
                if h % 2 == 0 and h >= 2:
                    pe.wait_ge(o_read, h // 2)
                p = pT[h % 2]
                v = [vv[:, m, h * HD:(h + 1) * HD] for m in range(MT)]
                mm(O_BANK[r, 0:P], v[0], p[:, 0, :], start=True, stop=True)
                mm(O_BANK[r, P:T], v[0], p[:, 1, :], start=True, stop=False)
                mm(O_BANK[r, P:T], v[1], p[:, 2, :], start=False, stop=True).then_inc(pv_done, 1)

            def qk_transposes():
                pe.wait_ge(qk_scaled, 2)
                for j in range(4):
                    i, m = divmod(j, 2)
                    for c in range(KC):
                        ins = nc.tensor.transpose(bank[4 + j][:, c * P:(c + 1) * P], (qn, kn)[i][:, m, c * P:(c + 1) * P], ident[:])
                    ins.then_inc(qkT_full, 1)

            def between(i):
                if i == SCORES - 1:
                    qk_transposes()
                if 0 <= i - SCORES < HEADS:
                    scores(i - SCORES)
                if 0 <= i - SCORES - 3 < HEADS:
                    transposed_probs(i - SCORES - 3)
                if i == 11:
                    pe.wait_ge(cv_done, 1)
                    claim(U_MEAN)
                    product(bank[U_MEAN % 4][:, 0:T], lambda k: ones[:], lambda k: cv[:, k, :], KC).then_inc(bank_full[U_MEAN % 4], 1)
                if i == 13:
                    pe.wait_ge(sqr_ready, 1)
                    claim(U_VAR)
                    product(bank[U_VAR % 4][:, 0:T], lambda k: ones[:], lambda k: sq[:, k, :], KC).then_inc(bank_full[U_VAR % 4], 1)
                if 0 <= i - SCORES - 4 < HEADS:
                    if i == SCORES + 4:
                        freed(pe, U_G + 8)
                        freed(pe, U_G + 9)
                    attend(i - SCORES - 4)

            for i in range(5, GROUPS):
                for b in range(2):
                    slot = 4 * (i - 5) + 2 * b
                    channel_group_bank(i, b, lambda: between(slot))
                    between(slot + 1)

            def branch(i, base, src, b):
                if b % 2 == 0:
                    split(i, b // 2)
                w = w_parts(i)
                u = base + b
                claim(u)
                for c in range(2):
                    ch = 2 * b + c
                    ins = product3(bank[u % 4][:, c * T:(c + 1) * T], lambda a, k: w[a][:, k, ch * P:(ch + 1) * P],
                                   lambda a, k: src[a][:, k, :], KC)
                ins.then_inc(bank_full[u % 4], 1)

            pe.wait_ge(o_read, KC)
            for b in range(4):
                branch(ATT_W, U_ATT, ao_r, b)
            pe.wait_ge(cv_lo, 1)
            for b in range(4):
                branch(CONV_W, U_CONV, cv_r, b)
            token_group(OUT_W, U_OUT, lambda k: pe.wait_ge(mix_lo, k // 2 + 1))

            def transpose_h(m):
                freed(pe, U_OUT + m)
                freed(pe, U_OUT + 2 + m)
                for b in range(2):
                    u = U_U2T + 2 * m + b
                    claim(u)
                    for j in range(4):
                        k = 4 * b + j
                        ins = nc.tensor.transpose(bank[u % 4][:, j * P:(j + 1) * P], hx[:, m, k * P:(k + 1) * P], ident[:])
                    ins.then_inc(bank_full[u % 4], 1)

            def logits(m):
                for b in range(2):
                    freed(pe, U_U2T + 2 * m + b)
                return product(bank[U_LOG % 4][:, m * E:(m + 1) * E], lambda k: u2T[:, k, m * P:(m + 1) * P], lambda k: wr[:, k, :], KD)

            w = w_parts(OUT_W + 1)
            for b in range(2):
                split(OUT_W + 1, b)
            for m in range(MT):
                u = U_OUT + 2 + m
                claim(u)
                for b in range(2):
                    ins = product3(bank[u % 4][:, b * T:(b + 1) * T], lambda a, k: u_r[a][:, k, m * P:(m + 1) * P],
                                   lambda a, k: w[a][:, k, b * T:(b + 1) * T], KD)
                    if b == 1:
                        ins.then_inc(bank_full[u % 4], 1)
                    elif m == 1:
                        transpose_h(0)
            pe.wait_ge(small_in, 48)
            claim(U_LOG)
            logits(0)
            transpose_h(1)

            def seed(j):
                return mm(acc[j][:], ident[:], hx[:, j // 2, j % 2 * 512:(j % 2 + 1) * 512], start=True, stop=False, skip_group_check=True)

            seed(0)
            logits(1).then_inc(bank_full[U_LOG % 4], 1)
            seed(1)
            seed(2)
            def gather_part(k):
                for m in range(MT):
                    ins = mm(GA[:, k * SLOTS:(k + 1) * SLOTS], u2[:, m, k * P:(k + 1) * P], hot[:, m, :],
                             start=(m == 0), stop=(m == MT - 1))
                return ins

            pe.wait_ge(tab_ready, 1)
            claim(U_TAB)
            tb = bank[U_TAB % 4]
            mm(tb[:, 0:E], tri[:], msk[:, 0, :], start=True, stop=True)
            mm(tb[:, E:2 * E], ones[:], msk[:, 0, :], start=True, stop=False)
            mm(tb[:, E:2 * E], tri[:], msk[:, 1, :], start=False, stop=True)
            mm(tb[0:E, 2 * E:2 * E + 1], msk[:, 0, :], ones[:, 0:1], start=True, stop=False)
            mm(tb[0:E, 2 * E:2 * E + 1], msk[:, 1, :], ones[:, 0:1], start=False, stop=True).then_inc(bank_full[U_TAB % 4], 1)
            pe.wait_ge(wide_ready, 1)
            claim(U_WIDE)
            mm(bank[U_WIDE % 4][0:E, 0:1], tri[0:E, 0:E], wide[:], start=True, stop=True).then_inc(bank_full[U_WIDE % 4], 1)
            pe.wait_ge(gate_ready, 1)
            claim(U_GT)
            for m in range(MT):
                ins = mm(bank[U_GT % 4][0:E, m * P:(m + 1) * P], gate[:, m, :], ident[:], start=True, stop=True)
            ins.then_inc(bank_full[U_GT % 4], 1)
            seed(3).then_inc(seeded, 1)
            freed(pe, U_WIDE)
            claim(U_KEYS)
            mm(bank[U_KEYS % 4][0:E, 0:E], key[:, 3:4].to_broadcast([E, E]), ident[0:E, 0:E], start=True, stop=True).then_inc(bank_full[U_KEYS % 4], 1)
            pe.wait_ge(hot_ready, MT)
            pe.wait_ge(u2_ready, MT)
            for k in range(3):
                gather_part(k)
            freed(pe, U_KEYS)
            claim(U_TURN)
            o = bank[U_TURN % 4]
            mm(o[0:E, 0:1], at_turn[:, 0:E], exp_col[:, 0:1], start=True, stop=True)
            mm(o[0:E, 1:2], at_turn[:, 0:E], exp_col[:, 2:3], start=True, stop=False)
            mm(o[0:E, 1:2], at_turn[:, 1:E + 1], exp_col[:, 1:2], start=False, stop=True).then_inc(bank_full[U_TURN % 4], 1)
            gather_part(3)
            freed(pe, U_TURN)
            claim(U_ENDS)
            tiles, jump = by_turn[:, 0:1], by_turn[:, 1:2]
            mm(bank[U_ENDS % 4][0:E, 0:1], tri[0:E, 0:E], tiles, start=True, stop=False)
            mm(bank[U_ENDS % 4][0:E, 0:1], ident[0:E, 0:E], tiles, start=False, stop=True).then_inc(bank_full[U_ENDS % 4], 1)
            claim(U_ITEMS)
            ib = bank[U_ITEMS % 4]
            mm(ib[0:1, 0:E + 1], tiles, tri[0:E, 0:E + 1], start=True, stop=True)
            mm(ib[0:1, 192:192 + E], exp_col[:, 1:2], at_turn[:, 0:E], start=True, stop=True)
            gather_part(4)
            freed(pe, U_ENDS)
            mm(ib[0:1, 64:64 + ITEMS], jump, past, start=True, stop=True)
            mm(ib[0:1, 128:128 + ITEMS], tiles, past, start=True, stop=True).then_inc(bank_full[U_ITEMS % 4], 1)
            def scatter():
                for m in range(MT):
                    for half in range(2):
                        ins = mm(acc[2 * m + half][:], hotT[:, m, :], ys[:, half, :], start=False, stop=False, skip_group_check=True)
                ins.then_inc(scattered, 1)

            for k in range(5, KD):
                ins = gather_part(k)
            ins.then_inc(gathered, 1)
            pe.wait_ge(bias_ready, 1)
            pe.wait_ge(cum_ready, 1)
            places = [(b_[half * SLOTS:(half + 1) * SLOTS, :], (2 * g + half) * 512)
                      for g, b_ in enumerate((HG, HL)) for half in range(2)]
            with pe.Fori(0, E // 2) as pair:
                for a in range(2):
                    e = pe.snap(2 * pair + a)
                    first = pe.value_load(cum[0:1, bass.ds(e, 1)], min_val=0, max_val=ITEMS - 1)
                    end = pe.value_load(cum[0:1, bass.ds(e + 1, 1)], min_val=1, max_val=ITEMS - 1)
                    with pe.Fori(first, end) as n:
                        pe.wait_ge(xt_ready, n + 1)
                        for m in range(MT):
                            nc.tensor.transpose(GA[:, m * P:(m + 1) * P], hotg[:, m, :], ident[:])
                        mm(GA[:, T:T + 1], hotg[:, 0, :], gcur[:, 0:1], start=True, stop=False)
                        mm(GA[:, T:T + 1], hotg[:, 1, :], gcur[:, 1:2], start=False, stop=True)
                        for g, b_ in enumerate((HG, HL)):
                            mm(b_[:], sel[:], bias_r[:, g, :], start=True, stop=False, skip_group_check=True)
                        for k in range(KD):
                            pe.wait_ge(up_in[a][k], 16 * pair + 16)
                            for o, f in places:
                                ins = mm(o, XT[:, k, :], up[a][:, k, f:f + 512], start=False, stop=(k == KD - 1), skip_group_check=True)
                            ins.then_inc(up_done[k], 1)
                            if k == 1:
                                pe.wait_ge(y_ready, n + 1)
                                pe.wait_ge(hotT_ready, n + 1)
                                scatter()
                        pe.wait_ge(hot_ready, 7 * n + 7 + MT)
                        for k in range(6):
                            gather_part(k)

                        def transpose_act(c):
                            pe.wait_ge(act_ready, 2 * n + c + 1)
                            for i in (2 * c, 2 * c + 1):
                                ins = nc.tensor.transpose(ACT_T[c][:, i % 2 * P:(i % 2 + 1) * P], ACT_A[:, i * P:(i + 1) * P], ident[:])
                            ins.then_inc(actT_full, 1)

                        transpose_act(0)
                        gather_part(6)
                        gather_part(7).then_inc(gathered, 1)
                        for step, c in enumerate(DOWN_ORDER):
                            if step == 1:
                                transpose_act(1)
                            if step % 2 == 0:
                                pe.wait_ge(actT_ready, 2 * n + step // 2 + 1)
                            pe.wait_ge(down_in[c], 16 * e + 16)
                            for k in (2 * c, 2 * c + 1):
                                for half in range(2):
                                    ins = mm(YB[half * SLOTS:(half + 1) * SLOTS, :], actT[:, k % 4, (k // 4) * SLOTS:(k // 4 + 1) * SLOTS],
                                             down[:, k, half * 512:(half + 1) * 512], start=(k == 0), stop=(k == KD - 1), skip_group_check=True)
                            ins.then_inc(down_done[c], 1)
            for m in range(MT):
                for n in range(2):
                    mm(acc[2 * m + n][:], gT[:, m * P:(m + 1) * P], bdown[:, n * 512:(n + 1) * 512],
                       start=False, stop=False, skip_group_check=True)
            items = pe.value_load(cum[0:1, E:E + 1], min_val=1, max_val=ITEMS - 1)
            pe.wait_ge(y_ready, items + 1)
            pe.wait_ge(hotT_ready, items + 1)
            scatter()


_INS = ["x", "norm1_g", "w_in", "b_gates", "conv_dw", "conv_dw_b", "conv_ln_g", "conv_ln_b", "w_conv_out",
        "q_norm_g", "k_norm_g", "w_attn_out", "w_out", "norm2_g", "w_router", "b_router",
        "w_up_gate", "b_up_gate", "w_down", "b_down"]


def kernel(**inputs):
    import numpy as np
    import concourse.bacc as bacc
    from concourse.bass_utils import run_bass_kernel_spmd

    nc = bacc.Bacc("TRN2", target_bir_lowering=False, num_devices=1, dynamic_dma_scratch_size=1024)
    arrays, args = {}, []
    for name in _INS:
        a = np.ascontiguousarray(inputs[name])
        a = a.reshape(a.shape[1:])
        arrays["in_" + name] = a
        args.append(nc.dram_tensor("in_" + name, a.shape, mybir.dt.from_np(a.dtype), kind="ExternalInput").ap())
    result = nc.dram_tensor("out_0", (T, D), F32, kind="ExternalOutput").ap()
    hybrid_block(nc, *args, result)
    r = run_bass_kernel_spmd(nc, [arrays], core_ids=[0])
    return r.results[0]["out_0"].reshape(1, T, D)
```
